# Optimizing a Trainium2 kernel written in Bass

```python
import math
import jax, jax.numpy as jnp
from jax import lax
import numpy as np

D_MODEL = 2048
BATCH = 1
SEQ = 256
DEPTH = 1
DEC_BATCH = 1
DEC_SEQ = 32
PAST_LEN = 256

CHUNK = 64
D_SSM = D_MODEL // 2
SSM_GROUP = 16
N_SSM_GROUPS = D_SSM // SSM_GROUP
SSM_STATE = 64
DT_MIN = 0.001
DT_MAX = 0.1
D_CONV = D_MODEL // 2
CONV_WIDTH = 31
CONV_BUF = CONV_WIDTH - 1
N_EXP_GROUPS = 4
EXP_PER_GROUP = 8
N_EXPERTS = N_EXP_GROUPS * EXP_PER_GROUP
TOP_K_INNER = 2
D_EXPERT = D_MODEL // 8
EPS = 1e-6
IN_COLS = D_SSM + 2 * D_CONV + 2 * D_MODEL

kernel_name = "hybrid_s5_conformer_hmoe_stream_step"

def rmsnorm(x, g):
    xf = x.astype(jnp.float32)
    r = lax.rsqrt(jnp.mean(xf * xf, axis=-1, keepdims=True) + EPS)
    return (xf * r * g.astype(jnp.float32)).astype(x.dtype)

def layernorm(x, g, b):
    xf = x.astype(jnp.float32)
    mu = jnp.mean(xf, axis=-1, keepdims=True)
    xc = xf - mu
    r = lax.rsqrt(jnp.mean(xc * xc, axis=-1, keepdims=True) + EPS)
    return (xc * r * g.astype(jnp.float32) + b.astype(jnp.float32)).astype(x.dtype)

def s5_scan(u, s_re, s_im, lam_re, lam_im, log_dt, b_re, b_im, c_re, c_im, d_skip):
    f32 = jnp.float32
    n, l, _ = u.shape
    uf = u.astype(f32).reshape(n, l, N_SSM_GROUPS, SSM_GROUP)
    lr = lam_re.astype(f32)
    li = lam_im.astype(f32)
    dt = jnp.exp(log_dt.astype(f32))[:, None]
    mag = jnp.exp(lr * dt)
    ar = mag * jnp.cos(li * dt)
    ai = mag * jnp.sin(li * dt)
    den = lr * lr + li * li
    nr = ar - 1.0
    cr = (nr * lr + ai * li) / den
    ci = (ai * lr - nr * li) / den
    br = b_re.astype(f32)
    bi = b_im.astype(f32)
    bbr = cr[..., None] * br - ci[..., None] * bi
    bbi = cr[..., None] * bi + ci[..., None] * br
    xr = jnp.einsum('nlgh,gph->nlgp', uf, bbr)
    xi = jnp.einsum('nlgh,gph->nlgp', uf, bbi)
    sr = s_re.astype(f32)
    si = s_im.astype(f32)
    xr = xr.at[:, 0].add(ar * sr - ai * si)
    xi = xi.at[:, 0].add(ar * si + ai * sr)
    a_r = jnp.broadcast_to(ar, xr.shape)
    a_i = jnp.broadcast_to(ai, xi.shape)

    def combine(e1, e2):
        a1r, a1i, b1r, b1i = e1
        a2r, a2i, b2r, b2i = e2
        return (a1r * a2r - a1i * a2i,
                a1r * a2i + a1i * a2r,
                a2r * b1r - a2i * b1i + b2r,
                a2r * b1i + a2i * b1r + b2i)

    _, _, hr, hi = lax.associative_scan(combine, (a_r, a_i, xr, xi), axis=1)
    y = (jnp.einsum('nlgp,ghp->nlgh', hr, c_re.astype(f32))
         - jnp.einsum('nlgp,ghp->nlgh', hi, c_im.astype(f32))
         + d_skip.astype(f32) * uf)
    return (y.reshape(n, l, D_SSM).astype(u.dtype),
            hr[:, -1].astype(u.dtype), hi[:, -1].astype(u.dtype))

def conv_branch(v, buf, conv_w, conv_b, ln_g, ln_b, w_conv_out):
    full = jnp.concatenate([buf.astype(v.dtype), v], axis=1)
    y = lax.conv_general_dilated(
        full, conv_w[:, None, :].astype(v.dtype), window_strides=(1,), padding='VALID',
        dimension_numbers=('NWC', 'WIO', 'NWC'), feature_group_count=D_CONV)
    y = y + conv_b.astype(v.dtype)
    y = jax.nn.silu(layernorm(y, ln_g, ln_b))
    return y @ w_conv_out.astype(v.dtype), full[:, -CONV_BUF:]

def mixer_block(x, s_re, s_im, buf, norm_mix_g, w_in, lam_re, lam_im, log_dt, b_re, b_im,
                c_re, c_im, d_skip, w_ssm_glu, conv_w, conv_b, conv_ln_g, conv_ln_b,
                w_conv_out, w_out):
    xn = rmsnorm(x, norm_mix_g)
    proj = xn @ w_in.astype(x.dtype)
    i1 = D_SSM
    i2 = i1 + D_CONV
    i3 = i2 + D_CONV
    i4 = i3 + D_MODEL
    u_ssm = proj[..., :i1]
    v_a = proj[..., i1:i2]
    v_b = proj[..., i2:i3]
    g_a = proj[..., i3:i4]
    g_b = proj[..., i4:]
    y_s, new_re, new_im = s5_scan(u_ssm, s_re, s_im, lam_re, lam_im, log_dt, b_re, b_im,
                                  c_re, c_im, d_skip)
    gl = jax.nn.gelu(y_s) @ w_ssm_glu.astype(x.dtype)
    y_a = gl[..., :D_MODEL] * jax.nn.sigmoid(gl[..., D_MODEL:])
    v = v_a * jax.nn.sigmoid(v_b)
    y_b, new_buf = conv_branch(v, buf, conv_w, conv_b, conv_ln_g, conv_ln_b, w_conv_out)
    m = jax.nn.sigmoid(g_a) * y_a + jax.nn.sigmoid(g_b) * y_b
    return x + m @ w_out.astype(x.dtype), new_re, new_im, new_buf

def hier_moe(x, norm_ffn_g, w_router_group, b_router_group, w_router_expert, b_router_expert,
             w_exp_gate, w_exp_up, w_exp_down):
    f32 = jnp.float32
    xn = rmsnorm(x, norm_ffn_g)
    lg = (xn @ w_router_group.astype(x.dtype)).astype(f32) + b_router_group.astype(f32)
    pg = jax.nn.softmax(lg, axis=-1)
    _, gsel = lax.top_k(lg, 1)
    pg_sel = jnp.take_along_axis(pg, gsel, axis=-1)
    le = (xn @ w_router_expert.astype(x.dtype)).astype(f32) + b_router_expert.astype(f32)
    le = le.reshape(le.shape[:-1] + (N_EXP_GROUPS, EXP_PER_GROUP))
    le_sel = jnp.take_along_axis(le, gsel[..., None], axis=-2)[..., 0, :]
    v2, i2 = lax.top_k(le_sel, TOP_K_INNER)
    w2 = jax.nn.softmax(v2, axis=-1) * pg_sel
    eid = gsel * EXP_PER_GROUP + i2
    gates = jnp.sum(jax.nn.one_hot(eid, N_EXPERTS, dtype=f32) * w2[..., None], axis=-2)
    hg = jnp.einsum('nld,edf->nlef', xn, w_exp_gate.astype(x.dtype))
    hu = jnp.einsum('nld,edf->nlef', xn, w_exp_up.astype(x.dtype))
    h = jax.nn.silu(hg) * hu * gates[..., None].astype(x.dtype)
    return x + jnp.einsum('nlef,efd->nld', h, w_exp_down.astype(x.dtype))

def setup_inputs(seed: int = 0) -> dict:
    key = jax.random.key(seed)
    ks = jax.random.split(key, 32)
    f32 = jnp.float32
    G, P, H = N_SSM_GROUPS, SSM_STATE, SSM_GROUP

    def nrm(k, shape, scale):
        return jax.random.normal(k, shape, f32) * scale

    lam_re = -0.5 + 0.01 * jax.random.uniform(ks[5], (DEPTH, G, P), f32, -1.0, 1.0)
    lam_im = (jnp.pi * jnp.arange(P, dtype=f32))[None, None, :] + nrm(ks[6], (DEPTH, G, P), 0.01)
    log_dt = jax.random.uniform(ks[7], (DEPTH, G), f32, math.log(DT_MIN), math.log(DT_MAX))
    return {
        "x_prompt": nrm(ks[0], (BATCH, SEQ, D_MODEL), 1.0),
        "x_sample": nrm(ks[1], (DEC_BATCH, DEC_SEQ, D_MODEL), 1.0),
        "state_ssm_re": nrm(ks[2], (DEPTH, DEC_BATCH, G, P), 0.1),
        "state_ssm_im": nrm(ks[3], (DEPTH, DEC_BATCH, G, P), 0.1),
        "cache_conv": nrm(ks[4], (DEPTH, DEC_BATCH, CONV_BUF, D_CONV), 0.5),
        "norm_mix_g": 1.0 + nrm(ks[8], (DEPTH, D_MODEL), 0.01),
        "w_in": nrm(ks[9], (DEPTH, D_MODEL, IN_COLS), D_MODEL ** -0.5),
        "lam_re": lam_re,
        "lam_im": lam_im,
        "log_dt": log_dt,
        "b_re": nrm(ks[10], (DEPTH, G, P, H), (2 * H) ** -0.5),
        "b_im": nrm(ks[11], (DEPTH, G, P, H), (2 * H) ** -0.5),
        "c_re": nrm(ks[12], (DEPTH, G, H, P), (2 * P) ** -0.5),
        "c_im": nrm(ks[13], (DEPTH, G, H, P), (2 * P) ** -0.5),
        "d_skip": nrm(ks[14], (DEPTH, G, H), 0.5),
        "w_ssm_glu": nrm(ks[15], (DEPTH, D_SSM, 2 * D_MODEL), D_SSM ** -0.5),
        "conv_w": nrm(ks[16], (DEPTH, CONV_WIDTH, D_CONV), CONV_WIDTH ** -0.5),
        "conv_b": nrm(ks[17], (DEPTH, D_CONV), 0.01),
        "conv_ln_g": 1.0 + nrm(ks[18], (DEPTH, D_CONV), 0.01),
        "conv_ln_b": nrm(ks[19], (DEPTH, D_CONV), 0.01),
        "w_conv_out": nrm(ks[20], (DEPTH, D_CONV, D_MODEL), D_CONV ** -0.5),
        "w_out": nrm(ks[21], (DEPTH, D_MODEL, D_MODEL), D_MODEL ** -0.5),
        "norm_ffn_g": 1.0 + nrm(ks[22], (DEPTH, D_MODEL), 0.01),
        "w_router_group": nrm(ks[23], (DEPTH, D_MODEL, N_EXP_GROUPS), D_MODEL ** -0.5),
        "b_router_group": nrm(ks[24], (DEPTH, N_EXP_GROUPS), 0.01),
        "w_router_expert": nrm(ks[25], (DEPTH, D_MODEL, N_EXPERTS), D_MODEL ** -0.5),
        "b_router_expert": nrm(ks[26], (DEPTH, N_EXPERTS), 0.01),
        "w_exp_gate": nrm(ks[27], (DEPTH, N_EXPERTS, D_MODEL, D_EXPERT), D_MODEL ** -0.5),
        "w_exp_up": nrm(ks[28], (DEPTH, N_EXPERTS, D_MODEL, D_EXPERT), D_MODEL ** -0.5),
        "w_exp_down": nrm(ks[29], (DEPTH, N_EXPERTS, D_EXPERT, D_MODEL), D_EXPERT ** -0.5),
        "norm_final_g": 1.0 + nrm(ks[30], (D_MODEL,), 0.01),
    }

def reference(x_prompt, x_sample, state_ssm_re, state_ssm_im, cache_conv, norm_mix_g, w_in,
              lam_re, lam_im, log_dt, b_re, b_im, c_re, c_im, d_skip, w_ssm_glu, conv_w,
              conv_b, conv_ln_g, conv_ln_b, w_conv_out, w_out, norm_ffn_g, w_router_group,
              b_router_group, w_router_expert, b_router_expert, w_exp_gate, w_exp_up,
              w_exp_down, norm_final_g):
    hp = x_prompt
    hs = x_sample
    n_p = x_prompt.shape[0]
    p_re, p_im, p_conv = [], [], []
    s_re_out, s_im_out, s_conv_out = [], [], []
    for l in range(DEPTH):
        mix_w = (norm_mix_g[l], w_in[l], lam_re[l], lam_im[l], log_dt[l], b_re[l], b_im[l],
                 c_re[l], c_im[l], d_skip[l], w_ssm_glu[l], conv_w[l], conv_b[l],
                 conv_ln_g[l], conv_ln_b[l], w_conv_out[l], w_out[l])
        moe_w = (norm_ffn_g[l], w_router_group[l], b_router_group[l], w_router_expert[l],
                 b_router_expert[l], w_exp_gate[l], w_exp_up[l], w_exp_down[l])
        z_state = jnp.zeros((n_p, N_SSM_GROUPS, SSM_STATE), hp.dtype)
        z_buf = jnp.zeros((n_p, CONV_BUF, D_CONV), hp.dtype)
        hp, nre, nim, nbuf = mixer_block(hp, z_state, z_state, z_buf, *mix_w)
        hp = hier_moe(hp, *moe_w)
        p_re.append(nre)
        p_im.append(nim)
        p_conv.append(nbuf)
        hs, sre, sim, sbuf = mixer_block(hs, state_ssm_re[l], state_ssm_im[l], cache_conv[l], *mix_w)
        hs = hier_moe(hs, *moe_w)
        s_re_out.append(sre)
        s_im_out.append(sim)
        s_conv_out.append(sbuf)
    y_prompt = rmsnorm(hp, norm_final_g)
    y_sample = rmsnorm(hs, norm_final_g)
    return (y_prompt, y_sample, jnp.stack(p_re), jnp.stack(p_im), jnp.stack(p_conv),
            jnp.stack(s_re_out), jnp.stack(s_im_out), jnp.stack(s_conv_out))


_drawn_inputs = setup_inputs


def setup_inputs(seed=0):
    import zlib

    import numpy as np

    out = dict(_drawn_inputs(seed))
    spreads = {}
    factors = {'norm_mix_g': 3.91,
     'lam_re': 33.87,
     'c_re': 5.416,
     'c_im': 3.533,
     'conv_b': 5.311,
     'conv_ln_b': 6.842,
     'b_router_group': 5.712,
     'b_router_expert': 4.861,
     'norm_final_g': 30.627,
     'conv_ln_g': 4.081,
     'norm_ffn_g': 3.192}
    for name, (base, spread) in spreads.items():
        noise = np.random.default_rng([zlib.crc32(name.encode()), seed]).standard_normal(out[name].shape)
        drawn = base * np.exp(spread * noise) if base else spread * noise
        out[name] = __import__('jax').numpy.asarray(drawn.astype(out[name].dtype))
    for name, factor in factors.items():
        out[name] = (out[name] * factor).astype(out[name].dtype)
    return out
```

```python
import math
from contextlib import ExitStack

import concourse.bass as bass
from concourse import mybir
from concourse.alu_op_type import AluOpType as ALU

F32 = mybir.dt.float32
I32 = mybir.dt.int32
ACT = mybir.ActivationFunctionType
AX = mybir.AxisListType.X

P = 128
D = 2048
KD = D // P
DC = 1024
KC = DC // P
TP, TS = 256, 32
N = TP + TS
TOK, NT = 96, N // 96
G, PS, HC = 64, 64, 16
PAIRS = G // 2
QP = 4
TAPS = 31
PAD = TAPS - 1
VW = PAD + TP + PAD + TS
CW = VW - PAD
SMP = PAD + TP
EXPERTS, EG, EPG, FE = 32, 4, 8, 256
SLOTS = 2 * N
NARROW, WIDE = 96, N
XW_COLS = 800
assert SLOTS - (NARROW + 1) + WIDE <= XW_COLS
EPS = 1e-6
ROUND = 12582912.0
TWO_PI_1 = 6.28125
TWO_PI_2 = float(int((2 * math.pi - TWO_PI_1) * 2 ** 20) / 2 ** 20)
TWO_PI_3 = 2 * math.pi - TWO_PI_1 - TWO_PI_2
SLOT = 4096


class Slots:

    def __init__(self):
        self.fills = [0, 0, 0]

    def use(self, slot):
        self.fills[slot] += 1
        return self.fills[slot] - 1

    def loop(self, plan, turns):
        first = [self.fills[s] for s in plan]
        for s in plan:
            self.fills[s] += turns
        assert len(set(plan)) == len(plan)
        return first


class Chain:

    def __init__(self, eng, sem):
        self.eng, self.sem, self.n, self.turn = eng, sem, 0, 0

    def __call__(self, ins):
        self.n += 1
        ins.then_inc(self.sem, 1)
        self.eng.wait_ge(self.sem, self.turn + self.n)

    def enter(self, i, per_turn):
        self.turn, self.start, self.per_turn = i * per_turn, self.n, per_turn

    def leave(self, turns):
        assert self.n - self.start == self.per_turn, self.n - self.start
        self.n = self.start + turns * self.per_turn
        self.turn = 0


def build(nc, i_, o_, xt_dram, slots_dram):
    ctx = ExitStack()
    with ctx:
        arena = ctx.enter_context(nc.sbuf_tensor("arena", [P, 53000], F32))
        pb = ctx.enter_context(nc.psum_tensor("pb", [P, 8, 512], F32))
        made = {}

        def sem(name):
            if name not in made:
                made[name] = ctx.enter_context(nc.semaphore(name))
            return made[name]

        def at(off, *shape, rows=P):
            size = math.prod(shape)
            v = arena[0:rows, off:off + size]
            if len(shape) == 2:
                v = v.rearrange("p (a b) -> p a b", b=shape[1])
            if len(shape) == 3:
                v = v.rearrange("p (a b c) -> p a b c", b=shape[1], c=shape[2])
            return v

        RING = [s * SLOT for s in range(3)]
        IDENT, ONES, CV, TRI = 12288, 12416, 12544, 13016
        WR, RB = 13112, 13688
        FO = 13828
        S1F = 14340
        IDX = 14352
        CNTI, OFFI = 14364, 14396
        MAG, INJ = 14428, 14460
        FIN = 14524
        PAR = 14652
        REV = 14660
        XN, SG, UT, VP, ALLW = 14888, 19496, 28712, 31016, 33800
        XRI, E, DEC, W, T = 37896, 40200, 42504, 43656, 45960
        ACC, UCUR, BCUR, CCUR = 47112, 47430, 47718, 47974
        ACC2 = 52326
        EL, SBT = 48230, 50278
        PT = 50278
        XNAT = 37896
        XT = SG
        ROWS, LD, BR, CR, CACHE = 44400, 44912, 44928, 45952, 46976
        SPA = 37896
        BBP, CPAD = 40200, 42248
        VOUT = SG + 4608
        YB, MU = 33800, 36104
        SBT2, SQ, MT, HT = 37896, 39048, 42504, 48392
        XNT, OH, GW, TMP, XG, Y = 19496, 25640, 27368, 29096, 30824, 14888
        GATE, XW, IOT, HID, RT = 43624, 44424, 44424, 45960, 45960
        HN, GF, YG = 30824, 36968, 14888

        ident, ones, tri = at(IDENT, P), at(ONES, P), at(TRI, TOK, rows=TOK)
        cv = at(CV, 472)
        c_mix, c_ffn, c_cb, c_lg, c_lb, c_ds = 0, 16, 32, 40, 48, 56
        c_lr, c_li, c_dt, c_sr, c_si, c_cw = 64, 96, 128, 160, 192, 224
        xn, xt, ht = at(XN, KD, N), at(XT, KD, N), at(HT, KD, N)
        sg, ut, vp = at(SG, 2 * KD, N), at(UT, KC, N), at(VP, KC, VW)
        mt = at(MT, KD, N)
        ring = [at(r, SLOT) for r in RING]

        block = ctx.enter_context(nc.Block())
        w_in = i_["w_in"][0]

        def cols(w, c0, width):
            return w[:, bass.ds(c0, width)].rearrange("(k p) c -> p k c", p=P)

        def slot_view(s, width):
            return ring[s].rearrange("p (k c) -> p k c", c=width)

        U_PLAN = [0, 1, 2, 0]
        V_PLAN, G_PLAN, GLU_PLAN, CO_PLAN, WO_PLAN, EXP_PLAN = [2, 1], [0, 1], [2, 0], [1, 2], [0, 1], [2, 0, 1]
        plan = Slots()
        u_fill = [plan.use(s) for s in U_PLAN]
        v_fill = plan.loop(V_PLAN, 4)
        g_fill = plan.loop(G_PLAN, 8)
        glu_fill = plan.loop(GLU_PLAN, 4)
        co_fill = plan.loop(CO_PLAN, 2)
        wo_fill = plan.loop(WO_PLAN, 4)
        exp_fill = plan.loop(EXP_PLAN, EXPERTS)
        FIRST = {
            "pe": ("x_done0", "x_done1", "c_done", "down_done"),
            "act": ("vb_out", "x_out0", "x_out1", "g_out", "glub_out", "down_act"),
            "dve": ("v_done", "rot_done", "ys_done", "glua_out", "glu_m", "co_out0", "co_out1", "wo_out0", "wo_out1",
                    "down_dve"),
        }

        def first_slot(eng, e, wide):
            return eng.value_load(at(OFFI, EXPERTS, rows=1).bitcast(I32)[0:1, bass.ds(e, 1)], min_val=0,
                                  max_val=SLOTS - (NARROW + 1) if wide else SLOTS)

        @block.sync
        def _(sp):
            slots = Slots()

            def load(s, fill, src, width):
                sp.wait_ge(sem(f"block_done{s}"), fill)
                sp.dma_start(slot_view(s, width), src).then_inc(sem(f"slot_full{s}"), 16)

            x_p, x_s = i_["x_prompt"][0], i_["x_sample"][0]
            nat = at(XNAT, NT, D, rows=TOK)
            sp.dma_start(nat[:, 0, :], x_p[0:96, :]).then_inc(sem("x_in"), 16)
            sp.dma_start(nat[:, 1, :], x_p[96:192, :]).then_inc(sem("x_in"), 16)
            sp.dma_start(nat[0:64, 2, :], x_p[192:256, :]).then_inc(sem("x_in"), 16)
            sp.dma_start(nat[64:96, 2, :], x_s[:, :]).then_inc(sem("x_in"), 16)
            for b, s in enumerate(U_PLAN[:3]):
                load(s, slots.use(s), cols(w_in, b * 256, 256), 256)
            sp.wait_ge(sem("xt_act"), 4)
            sp.wait_ge(sem("xt_dve"), 4)
            sp.dma_start(xt_dram, at(XT, KD * N)).then_inc(sem("xt_out"), 16)
            load(0, slots.use(0), cols(w_in, 3 * 256, 256), 256)
            f = slots.loop([2, 1], 4)
            with sp.Fori(0, 4) as i:
                load(2, f[0] + i, cols(w_in, i * 256 + 2 * DC, 256), 256)
                load(1, f[1] + i, cols(w_in, i * 256 + DC, 256), 256)
            f = slots.loop([0, 1], 8)
            with sp.Fori(0, 8) as i:
                load(0, f[0] + i, cols(w_in, i * 512 + 3 * DC, 256), 256)
                load(1, f[1] + i, cols(w_in, i * 512 + 3 * DC + 256, 256), 256)
            glu = i_["w_ssm_glu"][0]
            f = slots.loop([2, 0], 4)
            with sp.Fori(0, 4) as i:
                load(2, f[0] + i, cols(glu, i * 512, 512), 512)
                load(0, f[1] + i, cols(glu, i * 512 + D, 512), 512)
            sp.dma_start(at(HT, KD * N), xt_dram).then_inc(sem("ht_in"), 16)
            wco = i_["w_conv_out"][0]
            f = slots.loop([1, 2], 2)
            with sp.Fori(0, 2) as i:
                load(1, f[0] + i, cols(wco, i * 1024, 512), 512)
                load(2, f[1] + i, cols(wco, i * 1024 + 512, 512), 512)
            wo = i_["w_out"][0]
            f = slots.loop([0, 1], 4)
            with sp.Fori(0, 4) as i:
                load(0, f[0] + i, cols(wo, i * 512, 256), 256)
                load(1, f[1] + i, cols(wo, i * 512 + 256, 256), 256)
            gate, up, down = i_["w_exp_gate"][0], i_["w_exp_up"][0], i_["w_exp_down"][0]
            f = slots.loop([2, 0, 1], EXPERTS)
            sp.wait_ge(sem("block_done1"), exp_fill[2])
            with sp.Fori(0, EXPERTS) as e:
                load(2, f[0] + e, gate[bass.ds(e, 1)].rearrange("e (k p) c -> p (e k) c", p=P), FE)
                load(0, f[1] + e, up[bass.ds(e, 1)].rearrange("e (k p) c -> p (e k) c", p=P), FE)
                sp.wait_ge(sem("down_done"), 1 + e * KD)
                sp.dma_start(slot_view(1, D), down[bass.ds(e, 1)].rearrange("e (k p) c -> p (e k) c", p=P)).then_inc(sem("slot_full1"), 16)
            rows = arena[0:TOK, 0:12288].rearrange("p (s c) -> p s c", c=D)
            for s in range(SLOTS // TOK):
                sp.wait_ge(sem("row_act"), 2 * (s + 1))
                sp.wait_ge(sem("row_dve"), 2 * (s + 1))
                sp.dma_start(slots_dram[s * TOK:(s + 1) * TOK, :], rows[:, s, :]).then_inc(sem("slots_out"), 16)
            o = at(YG, NT, 2, D, rows=TOK)
            for j in range(NT):
                sp.wait_ge(sem("y_done"), j + 1)
                if j < 2:
                    sp.dma_start(o_["y_prompt"][0, j * TOK:(j + 1) * TOK, :], o[:, j, 0, :]).then_inc(sem("out_sp"), 16)
                else:
                    sp.dma_start(o_["y_prompt"][0, 192:256, :], o[0:64, j, 0, :]).then_inc(sem("out_sp"), 16)
                    sp.dma_start(o_["y_sample"][0], o[64:96, j, 0, :]).then_inc(sem("out_sp"), 16)
            sp.wait_ge(sem("out_sp"), 64)

        @block.gpsimd
        def _(po):
            chain = Chain(po, sem("po_chain"))
            po.memset(ident, 0.0).then_inc(sem("po_chain"), 1)
            po.memset(tri, 1.0).then_inc(sem("po_chain"), 1)
            po.memset(ones, 1.0).then_inc(sem("consts"), 1)
            chain.n += 2
            po.wait_ge(sem("po_chain"), 2)
            po.affine_select(out=ident, in_=ident, compare_op=ALU.not_equal, fill=1.0, base=0,
                             pattern=[[-1, P]], channel_multiplier=1).then_inc(sem("consts"), 1)
            po.affine_select(out=tri, in_=tri, compare_op=ALU.is_gt, fill=0.0, base=0,
                             pattern=[[1, TOK]], channel_multiplier=-1).then_inc(sem("consts"), 1)
            po.iota(at(REV, EXPERTS).bitcast(I32), pattern=[[-1, EXPERTS]], base=EXPERTS,
                    channel_multiplier=0).then_inc(sem("consts"), 1)
            po.iota(at(PAR, 1).bitcast(I32), pattern=[[0, 1]], base=0,
                    channel_multiplier=1).then_inc(sem("consts"), 1)
            po.memset(vp[:, :, 0:PAD], 0.0).then_inc(sem("vp_pad"), 1)
            po.wait_ge(sem("v_done"), 1 + 4)
            po.wait_ge(sem("prep_done"), 1)
            dec = at(DEC, QP, N)
            chain(po.memset(dec, 0.0))
            elr, eli = at(EL, PAIRS, 16), at(EL + 512, PAIRS, 16)
            ehr, ehi = at(EL + 1024, PAIRS, 16), at(EL + 1536, PAIRS, 16)
            er, ei = at(E, QP, N), at(E + QP * N, QP, N)
            pt, pt2 = at(PT, QP, 16, 16), at(PT + 1024, QP, 16, 16)
            er4 = er[:, :, 0:TP].rearrange("p q (a b) -> p q a b", b=16)
            ei4 = ei[:, :, 0:TP].rearrange("p q (a b) -> p q a b", b=16)
            po.wait_ge(sem("w_free"), 1)
            with po.Fori(0, KC) as i:
                chain.enter(i, 4)
                hi = [t[:, bass.ds(i * QP, QP), :].unsqueeze(3).to_broadcast([P, QP, 16, 16]) for t in (ehr, ehi)]
                lo = [t[:, bass.ds(i * QP, QP), :].unsqueeze(2).to_broadcast([P, QP, 16, 16]) for t in (elr, eli)]
                po.wait_ge(sem("rot_done"), 1 + i)
                po.tensor_tensor(er4, hi[0], lo[0], ALU.mult)
                po.tensor_tensor(pt, hi[1], lo[1], ALU.mult).then_inc(sem("po_chain"), 1)
                po.tensor_tensor(ei4, hi[0], lo[1], ALU.mult)
                po.tensor_tensor(pt2, hi[1], lo[0], ALU.mult).then_inc(sem("po_chain"), 1)
                chain.n += 2
                po.wait_ge(sem("po_chain"), chain.turn + chain.n)
                po.tensor_tensor(er4, er4, pt, ALU.subtract).then_inc(sem("po_chain"), 1)
                po.tensor_tensor(ei4, ei4, pt2, ALU.add).then_inc(sem("po_chain"), 1)
                chain.n += 2
                po.wait_ge(sem("po_chain"), chain.turn + chain.n)
                one = ones[:, 0:TS].unsqueeze(1).to_broadcast([P, QP, TS])
                po.tensor_tensor(er[:, :, TP:N], er[:, :, 0:TS], one, ALU.mult).then_inc(sem("tab_ready"), 1)
                po.tensor_tensor(ei[:, :, TP:N], ei[:, :, 0:TS], one, ALU.mult).then_inc(sem("tab_ready"), 1)
                mag = at(MAG, PAIRS)[:, bass.ds(i * QP, QP)].unsqueeze(2)
                po.tensor_copy(dec[:, :, 1:TP], mag.to_broadcast([P, QP, TP - 1])).then_inc(sem("tab_ready"), 1)
                po.tensor_copy(dec[:, :, TP + 1:N], mag.to_broadcast([P, QP, TS - 1])).then_inc(sem("tab_ready"), 1)
            chain.leave(KC)

            po.wait_ge(sem("block_done1"), wo_fill[1] + 4)
            po.iota(at(IOT, SLOTS, rows=TOK).bitcast(I32), pattern=[[1, SLOTS]], base=0,
                    channel_multiplier=0).then_inc(sem("iota_done"), 1)
            xg = at(XG, KD, XW_COLS)
            po.memset(xg[:, :, SLOTS:XW_COLS], 0.0).then_inc(sem("xg_pad"), 1)
            po.memset(at(GATE, XW_COLS)[:, SLOTS:XW_COLS], 0.0).then_inc(sem("xg_pad"), 1)
            po.wait_ge(sem("xg_act"), KD)
            po.wait_ge(sem("xg_dve"), KD)
            po.wait_ge(sem("route_done"), 1)
            with po.Fori(0, EXPERTS) as e:
                off = po.value_load(at(OFFI, EXPERTS, rows=1).bitcast(I32)[0:1, bass.ds(e, 1)],
                                    min_val=0, max_val=SLOTS)
                po.wait_ge(sem("block_done0"), exp_fill[1] + e)
                po.tensor_copy(at(XW, KD, NARROW), xg[:, :, bass.ds(off, NARROW)]).then_inc(sem("xw_ready"), 1)

            po.wait_ge(sem("slots_out"), 16 * (SLOTS // TOK))
            idx = at(IDX, 2, NT, rows=TOK).bitcast(I32)
            yg = at(YG, NT, 2, D, rows=TOK)
            for j in range(NT):
                for r in range(2):
                    po.indirect_dma_start(
                        out=yg[:, j, r, :], out_offset=None, in_=slots_dram[:, :],
                        in_offset=bass.IndirectOffsetOnAxis(ap=idx[:, r, j:j + 1], axis=0),
                    ).then_inc(sem(f"rows_in{j}"), 16)

        @block.tensor
        def _(pe):
            for name in FIRST["pe"]:
                pe.sem_inc(sem(name), 1)
            slots = Slots()

            def mm(out, lhsT, rhs, first, last):
                return pe.matmul(out, lhsT, rhs, start=first, stop=last)

            def products(s, fill, kt, width, rhs, outs, each=None):
                pe.wait_ge(sem(f"slot_full{s}"), (fill + 1) * 16)
                w = slot_view(s, width)
                for c, out in enumerate(outs):
                    for k in range(kt):
                        last = mm(out, w[:, k, c * P:(c + 1) * P], rhs[:, k, :], k == 0, k == kt - 1)
                last.then_inc(sem(f"block_done{s}"), 1)
                return last

            pe.wait_ge(sem("consts"), 5)
            pe.wait_ge(sem("x_in"), 64)
            nat = arena[0:TOK, XNAT:XNAT + NT * D].rearrange(
                "p (j k c) -> p j k c", j=NT, c=P)
            for m in range(KD // 2):
                b = 2 * (m % 2)
                if m >= 2:
                    pe.wait_ge(sem("xt_act" if m % 2 == 0 else "xt_dve"), m // 2)
                for kk in range(2):
                    for j in range(NT):
                        last = pe.transpose(pb[:, b + kk, j * TOK:(j + 1) * TOK], nat[:, j, 2 * m + kk, :],
                                            ident[0:TOK, 0:TOK])
                last.then_inc(sem("xt_t"), 1)

            def column_sums(src, bank, kt, width, ready, out, per_wait=1):
                for k in range(kt):
                    if k % per_wait == 0:
                        pe.wait_ge(ready[0], ready[1] + k // per_wait + 1)
                    last = mm(pb[:, bank, 0:width], ones, src[:, k, 0:width], k == 0, k == kt - 1)
                last.then_inc(out, 1)

            column_sums(xn, 5, KD, N, (sem("sq1"), 0), sem("ms1"), per_wait=4)

            pe.wait_ge(sem("rows_in"), 16 * 12)
            pe.wait_ge(sem("dt_rows"), 1)
            o = 0
            for n, r in enumerate((P, TOK, 124, 124)):
                last = pe.transpose(pb[:, 4, o:o + r], at(ROWS + n * P, P, rows=r), ident[0:r, 0:r])
                o += r
            last.then_inc(sem("cv_t"), 1)
            pe.wait_ge(sem("bc_in"), 16 * 5)
            for c in range(KC):
                last = pe.transpose(pb[:, 6, c * PAD:(c + 1) * PAD], at(CACHE, KC, P, rows=PAD)[:, c, :],
                                    ident[0:PAD, 0:PAD])
            last.then_inc(sem("cache_t"), 1)
            pe.wait_ge(sem("xn_ready"), KD)
            for b, s in enumerate(U_PLAN):
                q = 2 * (b % 2)
                if b == 0:
                    pe.wait_ge(sem("xt_act"), 4)
                    pe.wait_ge(sem("xt_dve"), 4)
                if b >= 2:
                    pe.wait_ge(sem("u_out"), b - 1)
                products(s, slots.use(s), KD, 256, xn, [pb[:, q + c, 0:N] for c in range(2)])

            f = slots.loop([2, 1], 4)
            pe.wait_ge(sem("u_out"), 4)
            with pe.Fori(0, 4) as i:
                pe.wait_ge(sem("vb_out"), 1 + i)
                products(2, f[0] + i, KD, 256, xn, [pb[:, 2 + c, 0:N] for c in range(2)])
                pe.wait_ge(sem("v_done"), 1 + i)
                products(1, f[1] + i, KD, 256, xn, [pb[:, c, 0:N] for c in range(2)])
            pe.wait_ge(sem("bb_ready"), 1)
            pe.wait_ge(sem("cv_out"), 1)
            pe.wait_ge(sem("cache_out"), 1)
            for c in range(KC):
                b = 4 + c % 4
                if c >= 4:
                    pe.wait_ge(sem("allw_out"), c - 3)
                for h in range(2):
                    pe.transpose(pb[:, b, h * P:(h + 1) * P], at(BBP + h * 1024, KC, P)[:, c, :], ident)
                for h in range(2):
                    last = pe.transpose(pb[:, b, (2 + h) * P:(3 + h) * P], at(CPAD + h * 1024, KC, P)[:, c, :], ident)
                last.then_inc(sem("allw_t"), 1)
            pe.wait_ge(sem("allw_out"), KC)
            pe.wait_ge(sem("v_done"), 1 + 4)
            for g, t0 in enumerate((TP, VW - PAD)):
                for c in range(KC):
                    last = pe.transpose(pb[0:PAD, 4 + 2 * g + c // 4, (c % 4) * P:(c % 4 + 1) * P],
                                        vp[:, c, t0:t0 + PAD], ident)
                last.then_inc(sem("vout_t"), 1)
            pe.wait_ge(sem("vout_copied"), 2)

            f = slots.loop([0, 1], 8)
            h_re, h_im = at(W, QP, N), at(W + QP * N, QP, N)
            with pe.Fori(0, KC) as i:
                pe.wait_ge(sem("cur_ready"), i + 1)
                for q in range(QP):
                    for h in range(2):
                        pe.wait_ge(sem(f"x_out{h}"), 1 + i * QP + q)
                        last = mm(pb[:, 4 + h, 0:N], at(BCUR, 2, P)[32 * q:32 * q + 32, h, :],
                                  at(UCUR, N)[32 * q:32 * q + 32, :], True, True)
                        last.then_inc(sem(f"x_done{h}"), 1)
                for t in range(2):
                    pe.wait_ge(sem("g_out"), 1 + i * 2 + t)
                    products(t, f[t] + i, KD, 256, xn, [pb[:, 2 * t + c, 0:N] for c in range(2)])
                pe.wait_ge(sem("h_ready"), i + 1)
                pe.wait_ge(sem("ccur_ready"), i + 1)
                pe.wait_ge(sem("ys_done"), 1 + i)
                for q in range(QP):
                    mm(pb[32 * q:32 * q + 32, 6, 0:N], at(CCUR, 2, P)[:, 0, 32 * q:32 * q + 32], h_re[:, q, :], True, False)
                    last = mm(pb[32 * q:32 * q + 32, 6, 0:N], at(CCUR, 2, P)[:, 1, 32 * q:32 * q + 32], h_im[:, q, :], False, True)
                last.then_inc(sem("c_done"), 1)

            pe.wait_ge(sem("rot_done"), 1 + KC)
            for n in range(4):
                last = pe.transpose(pb[0:PAIRS, 5, n * P:(n + 1) * P], at(FIN, 4, PAIRS)[:, n, :], ident)
            last.then_inc(sem("fin_t"), 1)
            pe.wait_ge(sem("gelu_done"), 1)
            pe.wait_ge(sem("g_out"), 1 + 16)
            pe.wait_ge(sem("fin_out"), 1)
            f = slots.loop([2, 0], 4)

            def glu_quad(q, fill):
                pe.wait_ge(sem("glua_out"), 1 + q)
                products(2, f[0] + fill, KC, 512, ut, [pb[:, c, 0:N] for c in range(4)])
                pe.wait_ge(sem("glub_out"), 1 + q)
                products(0, f[1] + fill, KC, 512, ut, [pb[:, 4 + c, 0:N] for c in range(4)])

            glu_quad(0, 0)
            pe.wait_ge(sem("conv_done"), KC)
            pe.wait_ge(sem("glub_out"), 1 + 1)
            for c in range(KC):
                last = mm(pb[:, 7, 0:CW], ones, vp[:, c, 0:CW], c == 0, c == KC - 1)
            last.then_inc(sem("mean_done"), 1)
            pe.wait_ge(sem("mu_done"), 1)
            glu_quad(1, 1)
            pe.wait_ge(sem("sq_ln"), 1)
            pe.wait_ge(sem("glub_out"), 1 + 2)
            for c in range(KC):
                last = mm(pb[:, 4, 0:CW], ones, at(SQ, KC, CW)[:, c, :], c == 0, c == KC - 1)
            last.then_inc(sem("var_done"), 1)
            pe.wait_ge(sem("var_read"), 1)
            with pe.Fori(2, 4) as i:
                glu_quad(i, i)
            pe.wait_ge(sem("yb_done"), 1)
            pe.wait_ge(sem("glua_out"), 1 + 4)
            pe.wait_ge(sem("glub_out"), 1 + 4)
            f = slots.loop([1, 2], 2)
            with pe.Fori(0, 2) as i:
                for t in range(2):
                    pe.wait_ge(sem(f"co_out{t}"), 1 + i)
                    products(1 + t, f[t] + i, KC, 512, at(YB, KC, N), [pb[:, 4 * t + c, 0:N] for c in range(4)])
            pe.wait_ge(sem("co_out0"), 1 + 2)
            pe.wait_ge(sem("co_out1"), 1 + 2)
            f = slots.loop([0, 1], 4)
            pe.wait_ge(sem("m_done"), 1)
            with pe.Fori(0, 4) as i:
                for t in range(2):
                    pe.wait_ge(sem(f"wo_out{t}"), 1 + i)
                    products(t, f[t] + i, KD, 256, mt, [pb[:, 2 * t + c, 0:N] for c in range(2)])
            column_sums(xn, 4, KD, N, (sem("sq2"), 0), sem("ms2"), per_wait=4)

            pe.wait_ge(sem("xn2_ready"), KD)
            wr = at(WR, KD, EG + EXPERTS)
            pe.wait_ge(sem("wr_in"), 64)
            for j in range(NT):
                for k in range(KD):
                    last = mm(pb[0:TOK, 5, j * 36:(j + 1) * 36], xn[:, k, j * TOK:(j + 1) * TOK], wr[:, k, :],
                              k == 0, k == KD - 1)
            last.then_inc(sem("logits"), 1)
            for n in range(NT * 4):
                j, g = divmod(n, 4)
                b = (6, 7, 0, 1)[n % 4]
                if n >= 4:
                    pe.wait_ge(sem("xnt_act"), n - 3)
                elif n >= 2:
                    pe.wait_ge(sem("wo_out0"), 1 + 4)
                for c in range(4):
                    last = pe.transpose(pb[0:TOK, b, c * P:(c + 1) * P], xn[:, 4 * g + c, j * TOK:(j + 1) * TOK], ident)
                last.then_inc(sem("xnt_t"), 1)
            a = at(RT + 600, NT, EXPERTS, rows=TOK)
            pe.wait_ge(sem("assigned"), 1)
            for j in range(NT):
                for jj in range(j + 1):
                    mm(pb[0:TOK, 2, j * 32:(j + 1) * 32], tri if jj == j else ones[0:TOK, 0:TOK], a[:, jj, :],
                       jj == 0, jj == j)
            for j in range(NT):
                last = mm(pb[:, 3, 0:32], ones[0:TOK, :], a[:, j, :], j == 0, j == NT - 1)
            last.then_inc(sem("ranks"), 1)
            pe.wait_ge(sem("xnt_act"), NT * 4)
            pe.wait_ge(sem("onehot"), 1)
            xnt = at(XNT, NT, D, rows=TOK)
            for k in range(KD):
                for h in range(2):
                    b = 4 + 2 * (k % 2) + h
                    if k >= 2:
                        pe.wait_ge(sem("xg_act" if h == 0 else "xg_dve"), k - 1)
                    for j in range(NT):
                        last = mm(pb[:, b, 0:N], xnt[:, j, k * P:(k + 1) * P],
                                  at(OH, NT, SLOTS, rows=TOK)[:, j, h * N:(h + 1) * N], j == 0, j == NT - 1)
                    last.then_inc(sem(f"xg_mm{h}"), 1)
            pe.wait_ge(sem("gateweights"), 1)
            for h in range(2):
                for j in range(NT):
                    last = mm(pb[:, h, 0:N], ones[0:TOK, :], at(GW, NT, SLOTS, rows=TOK)[:, j, h * N:(h + 1) * N],
                              j == 0, j == NT - 1)
            last.then_inc(sem("gate_mm"), 1)
            pe.wait_ge(sem("gate_rows"), 2)

            f = slots.loop([2, 0, 1], EXPERTS)
            pe.wait_ge(sem("route_done"), 1)
            pe.wait_ge(sem("xg_act"), KD)
            pe.wait_ge(sem("xg_dve"), KD)
            pe.wait_ge(sem("xg_pad"), 2)
            with pe.Fori(0, EXPERTS) as e:
                cnt = pe.value_load(at(CNTI, EXPERTS, rows=1).bitcast(I32)[0:1, bass.ds(e, 1)], min_val=0, max_val=N)

                def expert(wide):
                    width = WIDE if wide else NARROW
                    hid = at(HID + 1152, 2, WIDE)
                    if wide:
                        off = first_slot(pe, e, wide)
                    pe.wait_ge(sem("xw_ready"), e + 1)
                    for s, base, fill in ((2, 0, f[0]), (0, 2, f[1])):
                        pe.wait_ge(sem(f"slot_full{s}"), (fill + e) * 16 + 16)
                        w = slot_view(s, FE)
                        for c in range(2):
                            out = pb[:, 4 + base + c, 0:WIDE] if wide else pb[:, 4, (base + c) * NARROW:(base + c + 1) * NARROW]
                            if not wide and base:
                                out = pb[:, 5, c * NARROW:(c + 1) * NARROW]
                            for k in range(KD):
                                rhs = at(XG, KD, XW_COLS)[:, k, bass.ds(off, WIDE)] if wide else at(XW, KD, NARROW)[:, k, :]
                                last = mm(out, w[:, k, c * P:(c + 1) * P], rhs, k == 0, k == KD - 1)
                        last.then_inc(sem(f"block_done{s}"), 1)
                    pe.wait_ge(sem("hid_done"), e + 1)
                    pe.wait_ge(sem("down_act"), 1 + e * 8)
                    pe.wait_ge(sem("down_dve"), 1 + e * 8)
                    pe.wait_ge(sem("slot_full1"), (f[2] + e) * 16 + 16)
                    w = slot_view(1, D)
                    for c in range(KD):
                        if wide:
                            out = pb[:, c % 2 if c < 8 else 2 + c % 2, 0:WIDE]
                            if c % 8 >= 2:
                                pe.wait_ge(sem("down_act" if c < 8 else "down_dve"), 1 + e * 8 + c % 8 - 1)
                        else:
                            out = pb[:, c // 4, (c % 4) * NARROW:(c % 4 + 1) * NARROW]
                        for k in range(2):
                            last = mm(out, w[:, k, c * P:(c + 1) * P], hid[:, k, 0:width], k == 0, k == 1)
                        if wide:
                            last.then_inc(sem("down_done"), 1)
                        elif c % 8 == 7:
                            last.then_inc(sem("down_done"), 8)

                with pe.If(cnt < NARROW + 1):
                    expert(False)
                with pe.Else():
                    expert(True)

            pe.wait_ge(sem("down_act"), 1 + EXPERTS * 8)
            pe.wait_ge(sem("down_dve"), 1 + EXPERTS * 8)
            for n in range(4 * (SLOTS // TOK + NT)):
                s, g = divmod(n, 4)
                if n >= 8:
                    pe.wait_ge(sem("row_act" if n % 2 == 0 else "row_dve"), n // 2 - 3)
                for c in range(4):
                    if s < SLOTS // TOK:
                        src = at(Y, KD, XW_COLS)[:, 4 * g + c, s * TOK:(s + 1) * TOK]
                    else:
                        j = s - SLOTS // TOK
                        src = ht[:, 4 * g + c, j * TOK:(j + 1) * TOK]
                    last = pe.transpose(pb[0:TOK, n % 8, c * P:(c + 1) * P], src, ident)
                last.then_inc(sem("row_t"), 1)

        @block.scalar
        def _(act):
            for name in FIRST["act"]:
                act.sem_inc(sem(name), 1)
            def row(tile, at_row, name, pattern="(r c) -> r c", c=P):
                src = i_[name]
                while len(src.shape) > 1:
                    src = src.rearrange("a b -> (a b)") if len(src.shape) == 2 else src[0] if src.shape[0] == 1 else src.rearrange(
                        "a b c -> (a b c)") if len(src.shape) == 3 else src
                n = src.shape[0] // P
                act.dma_start(at(ROWS + tile * P, P)[at_row:at_row + n, :], src.rearrange("(r c) -> r c", c=P))\
                    .then_inc(sem("rows_in"), 16)

            act.dma_start(at(LD, 2, rows=PAIRS), i_["log_dt"][0].rearrange("(r c) -> r c", c=2)).then_inc(sem("ld_in"), 16)
            row(0, 0, "norm_mix_g")
            row(0, 16, "norm_ffn_g")
            row(0, 32, "conv_b")
            row(0, 40, "conv_ln_g")
            row(0, 48, "conv_ln_b")
            row(0, 56, "d_skip")
            row(0, 64, "lam_re")
            row(0, 96, "lam_im")
            row(1, 32, "state_ssm_re")
            row(1, 64, "state_ssm_im")
            cw = i_["conv_w"][0].rearrange("k (c p) -> (k c) p", p=P)
            for t in range(2):
                act.dma_start(at(ROWS + (2 + t) * P, P, rows=124), cw[124 * t:124 * t + 124, :]).then_inc(sem("rows_in"), 16)
            act.dma_start(at(CACHE, DC, rows=PAD), i_["cache_conv"][0, 0]).then_inc(sem("bc_in"), 16)
            for h, name in enumerate(("b_re", "b_im")):
                act.dma_start(at(BR + 512 * h, PAIRS, HC), i_[name][0].rearrange("(r g) p h -> (g p) r h", g=2))\
                    .then_inc(sem("bc_in"), 16)
            for h, name in enumerate(("c_re", "c_im")):
                act.dma_start(at(CR + 512 * h, KC, PS), i_[name][0].rearrange("(t g) h p -> (g h) t p", g=8))\
                    .then_inc(sem("bc_in"), 16)
            wr = at(WR, KD, EG + EXPERTS)
            act.dma_start(wr[:, :, 0:EG], i_["w_router_group"][0].rearrange("(k p) c -> p k c", p=P)).then_inc(sem("wr_in"), 16)
            act.dma_start(wr[:, :, EG:EG + EXPERTS], i_["w_router_expert"][0].rearrange("(k p) c -> p k c", p=P)).then_inc(sem("wr_in"), 16)
            rb = at(RB, EG + EXPERTS, rows=TOK)
            act.dma_start(rb[:, 0:EG], i_["b_router_group"][0:1, :].to_broadcast([TOK, EG])).then_inc(sem("wr_in"), 16)
            act.dma_start(rb[:, EG:EG + EXPERTS], i_["b_router_expert"][0:1, :].to_broadcast([TOK, EXPERTS])).then_inc(sem("wr_in"), 16)

            for m in range(0, KD // 2, 2):
                act.wait_ge(sem("xt_t"), m + 1)
                act.activation(xt[:, 2 * m:2 * m + 2, :], pb[:, 0:2, 0:N], ACT.Copy).then_inc(sem("xt_act"), 1)

            def squares(src, n_ready, out):
                for g in range(4):
                    n_ready(g)
                    act.activation(xn[:, 4 * g:4 * g + 4, :], src[:, 4 * g:4 * g + 4, :], ACT.Square).then_inc(out, 1)

            def xt_ready(g):
                act.wait_ge(sem("xt_act"), g + 1)
                act.wait_ge(sem("xt_dve"), g + 1)

            squares(xt, xt_ready, sem("sq1"))
            act.wait_ge(sem("v1"), 1)
            act.activation(at(SBT + N, N), at(SBT, N), ACT.Sqrt).then_inc(sem("sd1"), 1)
            act.wait_ge(sem("cv_t"), 1)
            act.activation(cv, pb[:, 4, 0:472], ACT.Copy).then_inc(sem("cv_out"), 1)
            act.wait_ge(sem("cache_t"), 1)
            act.activation(vp[:, :, PAD + TP:2 * PAD + TP], pb[:, 6, 0:KC * PAD].rearrange("p (c t) -> p c t", t=PAD),
                           ACT.Copy).then_inc(sem("cache_out"), 1)
            act.wait_ge(sem("cv_out"), 1)
            act.activation(at(SPA, 32), cv[:, c_dt:c_dt + 32], ACT.Exp).then_inc(sem("dt_exp"), 1)
            act.wait_ge(sem("lrdt"), 1)
            act.activation(at(MAG, 32), at(SPA + 32, 32), ACT.Exp).then_inc(sem("mag"), 1)
            act.wait_ge(sem("angles"), 1)
            act.activation(at(SPA + 768, 256), at(SPA + 512, 256), ACT.Sin).then_inc(sem("sines"), 1)
            act.activation(at(SPA + 1024, 256), at(SPA + 512, 256), ACT.Sin, scale=0.5).then_inc(sem("sines"), 1)
            for b in range(4):
                act.wait_ge(sem(f"block_done{U_PLAN[b]}"), u_fill[b] + 1)
                act.activation(ut[:, 2 * b:2 * b + 2, :], pb[:, 2 * (b % 2):2 * (b % 2) + 2, 0:N], ACT.Copy)\
                    .then_inc(sem("u_out"), 1)
            with act.Fori(0, 4) as i:
                act.wait_ge(sem("block_done2"), v_fill[0] + i + 1)
                act.wait_ge(sem("v_done"), 1 + i)
                act.activation(at(SBT, 2, N), pb[:, 2:4, 0:N], ACT.Sigmoid).then_inc(sem("vb_out"), 1)
            for c in range(KC):
                act.wait_ge(sem("allw_t"), c + 1)
                act.activation(at(ALLW, KC, 512)[:, c, :], pb[:, 4 + c % 4, :], ACT.Copy).then_inc(sem("allw_out"), 1)
            act.wait_ge(sem("xt_out"), 16)
            for g in range(2):
                act.wait_ge(sem("vout_t"), g + 1)
                act.activation(arena[0:PAD, VOUT + g * DC:VOUT + (g + 1) * DC].rearrange("p (a b) -> p a b", b=512),
                               pb[0:PAD, 4 + 2 * g:6 + 2 * g, :], ACT.Copy).then_inc(sem("vout_copied"), 1)
            act.wait_ge(sem("vout_copied"), 2)
            act.dma_start(o_["conv_p"][0, 0], arena[0:PAD, VOUT:VOUT + DC]).then_inc(sem("vout"), 16)
            act.dma_start(o_["conv_s"][0, 0], arena[0:PAD, VOUT + DC:VOUT + 2 * DC]).then_inc(sem("vout"), 16)
            act.wait_ge(sem("vout"), 32)
            act.wait_ge(sem("w_free"), 1)
            act.wait_ge(sem("allw_out"), KC)
            xr, xi = at(XRI, QP, N), at(XRI + QP * N, QP, N)
            with act.Fori(0, KC) as i:
                act.wait_ge(sem("x_done0"), 1 + i * QP)
                act.wait_ge(sem("x_done1"), 1 + i * QP)
                act.activation(at(UCUR, N), ut[:, bass.ds(i, 1), :], ACT.Copy)
                act.activation(at(BCUR, 256), at(ALLW, KC, 512)[:, bass.ds(i, 1), 0:256], ACT.Copy).then_inc(sem("cur_ready"), 1)
                act.wait_ge(sem("rot_done"), 1 + i)
                for q in range(QP):
                    for h in range(2):
                        act.wait_ge(sem(f"x_done{h}"), 1 + i * QP + q + 1)
                        act.activation((xr, xi)[h][:, q, :], pb[:, 4 + h, 0:N], ACT.Copy).then_inc(sem(f"x_out{h}"), 1)
                for t in range(2):
                    act.wait_ge(sem(f"block_done{t}"), g_fill[t] + i + 1)
                    act.activation(sg[:, bass.ds(i * 4 + 2 * t, 2), :], pb[:, 2 * t:2 * t + 2, 0:N], ACT.Sigmoid)\
                        .then_inc(sem("g_out"), 1)
                    if t == 0:
                        act.wait_ge(sem("c_done"), 1 + i)
                        act.activation(at(CCUR, 256), at(ALLW, KC, 512)[:, bass.ds(i, 1), 256:512], ACT.Copy)\
                            .then_inc(sem("ccur_ready"), 1)
            act.wait_ge(sem("ys_done"), 1 + KC)
            act.activation(at(UT, KC * N), at(UT, KC * N), ACT.Gelu_apprx_tanh).then_inc(sem("gelu_done"), 1)
            act.wait_ge(sem("fin_t"), 1)
            act.activation(at(FO, 512, rows=PAIRS), pb[0:PAIRS, 5, :], ACT.Copy).then_inc(sem("fin_out"), 1)
            act.wait_ge(sem("fin_out"), 1)
            for n, name in enumerate(("re_p", "im_p", "re_s", "im_s")):
                act.dma_start(o_[name][0, 0].rearrange("(r g) p -> r (g p)", g=2), at(FO + n * P, P, rows=PAIRS))\
                    .then_inc(sem("fin_dma"), 16)

            def glu_gates(q):
                act.wait_ge(sem("block_done0"), glu_fill[1] + q + 1)
                act.wait_ge(sem("glu_m"), 1 + q)
                act.activation(at(SBT2, 4, N), pb[:, 4:8, 0:N], ACT.Sigmoid).then_inc(sem("glub_out"), 1)

            glu_gates(0)
            act.wait_ge(sem("xc_done"), 1)
            act.activation(at(SQ, KC, CW), vp[:, :, 0:CW], ACT.Square).then_inc(sem("sq_ln"), 1)
            glu_gates(1)
            act.wait_ge(sem("var_read"), 1)
            act.activation(at(MU + CW, CW), at(MU, CW), ACT.Sqrt).then_inc(sem("sd_ln"), 1)
            act.wait_ge(sem("z_done"), 1)
            act.activation(at(SQ, KC, CW), vp[:, :, 0:CW], ACT.Sigmoid).then_inc(sem("z_sig"), 1)
            with act.Fori(2, 4) as i:
                glu_gates(i)
            def ht_ready(g):
                act.wait_ge(sem("wo_out0"), 1 + g + 1)
                act.wait_ge(sem("wo_out1"), 1 + g + 1)

            squares(ht, ht_ready, sem("sq2"))
            act.wait_ge(sem("v2"), 1)
            act.activation(at(RT + N, N), at(RT, N), ACT.Sqrt).then_inc(sem("sd2"), 1)
            act.wait_ge(sem("xn2_ready"), KD)
            for n in range(NT * 4):
                j, g = divmod(n, 4)
                act.wait_ge(sem("xnt_t"), n + 1)
                act.activation(at(XNT, NT, D, rows=TOK)[:, j, g * 512:(g + 1) * 512], pb[0:TOK, (6, 7, 0, 1)[n % 4], :],
                               ACT.Copy).then_inc(sem("xnt_act"), 1)
            act.wait_ge(sem("rt_g"), 1)
            act.activation(at(RT + 120, 12, rows=TOK), at(RT + 108, 12, rows=TOK), ACT.Exp).then_inc(sem("rt_ge"), 1)
            act.wait_ge(sem("rt_d"), 1)
            act.activation(at(RT + 156, 3, rows=TOK), at(RT + 153, 3, rows=TOK), ACT.Exp).then_inc(sem("rt_de"), 1)
            xg = at(XG, KD, XW_COLS)
            for k in range(KD):
                act.wait_ge(sem("xg_mm0"), k + 1)
                act.activation(xg[:, k, 0:N], pb[:, 4 + 2 * (k % 2), 0:N], ACT.Copy).then_inc(sem("xg_act"), 1)
            act.wait_ge(sem("gate_mm"), 1)
            act.activation(at(GATE, N), pb[:, 0, 0:N], ACT.Copy).then_inc(sem("gate_rows"), 1)
            act.wait_ge(sem("route_done"), 1)
            y = at(Y, KD, XW_COLS)
            with act.Fori(0, EXPERTS) as e:
                cnt = act.value_load(at(CNTI, EXPERTS, rows=1).bitcast(I32)[0:1, bass.ds(e, 1)], min_val=0, max_val=N)

                def expert(wide):
                    width = WIDE if wide else NARROW
                    off = first_slot(act, e, wide)
                    act.wait_ge(sem("block_done2"), exp_fill[0] + e + 1)
                    src = pb[:, 4:6, 0:WIDE] if wide else pb[:, 4, 0:2 * NARROW].rearrange("p (c n) -> p c n", n=NARROW)
                    act.activation(at(HID, 2, WIDE)[:, :, 0:width], src, ACT.Sigmoid).then_inc(sem("sig_done"), 1)
                    if wide:
                        for c in range(8):
                            act.wait_ge(sem("down_done"), 1 + e * KD + c + 1)
                            act.activation(y[:, c, bass.ds(off, WIDE)], pb[:, c % 2, 0:WIDE], ACT.Copy)\
                                .then_inc(sem("down_act"), 1)
                    else:
                        act.wait_ge(sem("down_done"), 1 + e * KD + 8)
                        act.activation(y[:, 0:8, bass.ds(off, NARROW)].rearrange("p (b c) n -> p b c n", c=4),
                                       pb[:, 0:2, 0:4 * NARROW].rearrange("p b (c n) -> p b c n", n=NARROW),
                                       ACT.Copy).then_inc(sem("down_act"), 8)

                with act.If(cnt < NARROW + 1):
                    expert(False)
                with act.Else():
                    expert(True)

            def row_place(n):
                s, g = divmod(n, 4)
                if s < SLOTS // TOK:
                    return arena[0:TOK, s * D + g * 512:s * D + (g + 1) * 512]
                return arena[0:TOK, HN + (s - SLOTS // TOK) * D + g * 512:HN + (s - SLOTS // TOK) * D + (g + 1) * 512]

            for n in range(0, 4 * (SLOTS // TOK + NT), 2):
                act.wait_ge(sem("row_t"), n + 1)
                act.activation(row_place(n), pb[0:TOK, n % 8, :], ACT.Copy).then_inc(sem("row_act"), 1)
            gf = at(GF, D, rows=TOK)
            act.dma_start(gf, i_["norm_final_g"].unsqueeze(0).to_broadcast([TOK, D])).then_inc(sem("gf_in"), 16)
            yg = at(YG, NT, 2, D, rows=TOK)
            for j in range(NT):
                act.wait_ge(sem("sum_done"), j + 1)
                act.activation(yg[:, j, 1, :], yg[:, j, 0, :], ACT.Square, accum_out=at(RT + 4 * j, 1, rows=TOK)).then_inc(sem("ss_done"), 1)
                act.wait_ge(sem("vf"), j + 1)
                act.activation(at(RT + 4 * j + 1, 1, rows=TOK), at(RT + 4 * j, 1, rows=TOK), ACT.Sqrt).then_inc(sem("sdf"), 1)
            act.wait_ge(sem("vout"), 32)
            act.wait_ge(sem("fin_dma"), 64)

        @block.vector
        def _(dve):
            for name in FIRST["dve"]:
                dve.sem_inc(sem(name), 1)
            v = nc.vector
            chain = Chain(dve, sem("dve_chain"))
            dve.wait_ge(sem("ld_in"), 16)
            v.tensor_copy(at(ROWS + P, 2, PS, rows=PAIRS), at(LD, 2, rows=PAIRS).unsqueeze(2).to_broadcast([PAIRS, 2, PS]))\
                .then_inc(sem("dt_rows"), 1)
            for m in range(1, KD // 2, 2):
                dve.wait_ge(sem("xt_t"), m + 1)
                v.tensor_copy(xt[:, 2 * m:2 * m + 2, :], pb[:, 2:4, 0:N]).then_inc(sem("xt_dve"), 1)

            def root(total, size, var, scale, v_sem, sd_sem, extra=None):
                vv, sd, tt = var
                chain(v.tensor_scalar(vv, total, scale, EPS, ALU.mult, ALU.add))
                v_sem_ins = v.tensor_copy(tt, vv)
                v_sem_ins.then_inc(v_sem, 1)
                dve.wait_ge(sd_sem[0], sd_sem[1])
                chain(v.reciprocal(sd, sd))
                chain(v.tensor_tensor(tt, sd, sd, ALU.mult))
                chain(v.tensor_tensor(tt, tt, vv, ALU.mult))
                chain(v.tensor_scalar(tt, tt, -0.5, 1.5, ALU.mult, ALU.add))
                chain(v.tensor_tensor(sd, sd, tt, ALU.mult))
                return sd

            dve.wait_ge(sem("ms1"), 1)
            r = root(pb[:, 5, 0:N], N, [at(SBT + n * N, N) for n in range(3)], 1.0 / D, sem("v1"), (sem("sd1"), 1))
            dve.wait_ge(sem("cv_out"), 1)
            for k in range(KD):
                v.scalar_tensor_tensor(xn[:, k, :], xt[:, k, :], cv[:, c_mix + k:c_mix + k + 1], r, ALU.mult, ALU.mult)\
                    .then_inc(sem("xn_ready"), 1)

            dt, lrdt, mag = at(SPA, 32), at(SPA + 32, 32), at(MAG, 32)
            th, kf, ang = at(SPA + 64, 8, 32), at(SPA + 1280, 256), at(SPA + 512, 256)
            sn, cs = at(SPA + 768, 8, 32), at(SPA + 1024, 8, 32)
            lr, li = cv[:, c_lr:c_lr + 32], cv[:, c_li:c_li + 32]
            dve.wait_ge(sem("dt_exp"), 1)
            v.tensor_tensor(lrdt, lr, dt, ALU.mult).then_inc(sem("lrdt"), 1)
            chain(v.tensor_tensor(th[:, 0, :], li, dt, ALU.mult))
            for k in range(1, 8):
                chain(v.tensor_scalar(th[:, k, :], th[:, 0, :], float(2 ** k), None, ALU.mult))
            thf = at(SPA + 64, 256)
            chain(v.tensor_scalar(kf, thf, 1 / (2 * math.pi), ROUND, ALU.mult, ALU.add))
            chain(v.tensor_scalar(kf, kf, ROUND, None, ALU.subtract))
            chain(v.scalar_tensor_tensor(ang, kf, -TWO_PI_1, thf, ALU.mult, ALU.add))
            chain(v.scalar_tensor_tensor(ang, kf, -TWO_PI_2, ang, ALU.mult, ALU.add))
            chain(v.scalar_tensor_tensor(ang, kf, -TWO_PI_3, ang, ALU.mult, ALU.add))
            v.tensor_scalar(ang, ang, 3.1415925, -3.1415925, ALU.min, ALU.max).then_inc(sem("angles"), 1)
            dve.wait_ge(sem("sines"), 2)
            csf = at(SPA + 1024, 256)
            chain(v.tensor_tensor(csf, csf, csf, ALU.mult))
            chain(v.tensor_scalar(csf, csf, -2.0, 1.0, ALU.mult, ALU.add))
            dve.wait_ge(sem("mag"), 1)
            w = [at(SPA + 1536 + 32 * n, 32) for n in range(12)]
            ar, ai, t1, t2, den, nr, cr, ci = w[:8]
            chain(v.tensor_tensor(ar, mag, cs[:, 0, :], ALU.mult))
            chain(v.tensor_tensor(ai, mag, sn[:, 0, :], ALU.mult))
            s_r, s_i = cv[:, c_sr:c_sr + 32], cv[:, c_si:c_si + 32]
            for out, p1, q1, p2, q2, op in ((at(INJ, 32), ar, s_r, ai, s_i, ALU.subtract),
                                            (at(INJ + 32, 32), ar, s_i, ai, s_r, ALU.add),
                                            (den, lr, lr, li, li, ALU.add)):
                chain(v.tensor_tensor(t1, p1, q1, ALU.mult))
                chain(v.tensor_tensor(t2, p2, q2, ALU.mult))
                chain(v.tensor_tensor(out, t1, t2, op))
            chain(v.tensor_scalar(nr, ar, 1.0, None, ALU.subtract))
            chain(v.reciprocal(den, den))
            for out, p1, q1, p2, q2, op in ((cr, nr, lr, ai, li, ALU.add), (ci, ai, lr, nr, li, ALU.subtract)):
                chain(v.tensor_tensor(t1, p1, q1, ALU.mult))
                chain(v.tensor_tensor(t2, p2, q2, ALU.mult))
                chain(v.tensor_tensor(t1, t1, t2, op))
                chain(v.tensor_tensor(out, t1, den, ALU.mult))
            br, bi = at(BR, PAIRS, HC), at(BR + 512, PAIRS, HC)
            crb, cib = (x.unsqueeze(2).to_broadcast([P, PAIRS, HC]) for x in (cr, ci))
            g1, g2 = at(SPA, PAIRS, HC), at(SPA + 1792, PAIRS, HC)
            par_i = at(PAR, 1).bitcast(I32)
            dve.wait_ge(sem("consts"), 5)
            dve.wait_ge(sem("bc_in"), 16 * 5)
            first = v.memset(at(EL, 2048), 0.0)
            chain(first)
            for base in (0, 1024):
                chain(v.memset(at(EL + base, PAIRS, 16)[:, :, 0:1], 1.0))
                tr, ti = at(EL + base, PAIRS, 16), at(EL + base + 512, PAIRS, 16)
                for lv in range(4):
                    n = 2 ** lv
                    k = lv + (4 if base else 0)
                    kr, ki = (x[:, k, :].unsqueeze(2).to_broadcast([P, PAIRS, n]) for x in (cs, sn))
                    m1, m2 = at(SPA + 1792, PAIRS, n), at(SPA + 2048, PAIRS, n)
                    for dst, p1, p2, op in ((tr, kr, ki, ALU.subtract), (ti, ki, kr, ALU.add)):
                        chain(v.tensor_tensor(m1, tr[:, :, 0:n], p1, ALU.mult))
                        chain(v.tensor_tensor(m2, ti[:, :, 0:n], p2, ALU.mult))
                        chain(v.tensor_tensor(dst[:, :, n:2 * n], m1, m2, op))
            chain(v.memset(at(BBP, 2048), 0.0))
            for h, (p1, q1, p2, q2, op) in enumerate(((crb, br, cib, bi, ALU.subtract), (crb, bi, cib, br, ALU.add))):
                chain(v.tensor_tensor(g1, q1, p1, ALU.mult))
                chain(v.tensor_tensor(g2, q2, p2, ALU.mult))
                bb = at(BBP + 1024 * h, PAIRS, 32)
                for half in range(2):
                    rows = slice(64 * half, 64 * half + 64)
                    chain(v.tensor_tensor(bb[rows, :, HC * half:HC * half + HC], g1[rows], g2[rows], op))
            chain(v.tensor_scalar(par_i, par_i, 4, 1, ALU.logical_shift_right, ALU.bitwise_and))
            odd, even = at(PAR + 1, 1), at(PAR + 2, 1)
            chain(v.tensor_copy(odd, par_i))
            chain(v.tensor_scalar(even, odd, -1.0, 1.0, ALU.mult, ALU.add))
            for h in range(2):
                src = at(CR + 512 * h, KC, PS)
                for half, mask in enumerate((even, odd)):
                    chain(v.tensor_scalar(at(CPAD + 1024 * h, KC, P)[:, :, PS * half:PS * half + PS], src, mask,
                                          -1.0 if h else 1.0, ALU.mult, ALU.mult))
            v.memset(at(FIN, 128), 0.0).then_inc(sem("bb_ready"), 1)

            dve.wait_ge(sem("cache_out"), 1)
            with dve.Fori(0, 4) as i:
                dve.wait_ge(sem("vb_out"), 1 + i + 1)
                dve.wait_ge(sem("block_done1"), v_fill[1] + i + 1)
                sb = at(SBT, 2, N)
                v.tensor_tensor(vp[:, bass.ds(i * 2, 2), PAD:PAD + TP], pb[:, 0:2, 0:TP], sb[:, :, 0:TP], ALU.mult)
                v.tensor_tensor(vp[:, bass.ds(i * 2, 2), 2 * PAD + TP:VW], pb[:, 0:2, TP:N], sb[:, :, TP:N], ALU.mult)\
                    .then_inc(sem("v_done"), 1)
            dve.wait_ge(sem("allw_out"), KC)
            v.memset(at(W, 1), 0.0).then_inc(sem("prep_done"), 1)
            dve.wait_ge(sem("vout_copied"), 2)
            dve.wait_ge(sem("v_done"), 1 + 4)
            dve.wait_ge(sem("vp_pad"), 1)
            v.memset(at(W + 1, 1), 0.0).then_inc(sem("w_free"), 1)

            xr, xi = at(XRI, QP, N), at(XRI + QP * N, QP, N)
            er, ei = at(E, QP, N), at(E + QP * N, QP, N)
            wr_, wi_ = at(W, QP, N), at(W + QP * N, QP, N)
            tt = at(T, QP, N)
            fin = at(FIN, 2, 2, PAIRS)
            acc = at(ACC, CW)
            flat = lambda off: at(off, QP * N)
            with dve.Fori(0, KC) as i:
                chain.enter(i, 48)

                def turn(dst, a1, b1, a2, b2, op):
                    v.tensor_tensor(dst, a1, b1, ALU.mult).then_inc(sem("dve_chain"), 1)
                    chain.n += 1
                    chain(v.tensor_tensor(tt, a2, b2, ALU.mult))
                    chain(v.tensor_tensor(dst, dst, tt, op))

                dve.wait_ge(sem("x_out0"), 1 + i * QP + QP)
                dve.wait_ge(sem("x_out1"), 1 + i * QP + QP)
                dve.wait_ge(sem("tab_ready"), i * 4 + 4)
                dve.wait_ge(sem("c_done"), 1 + i)
                turn(wr_, xr, er, xi, ei, ALU.add)
                turn(wi_, xi, er, xr, ei, ALU.subtract)
                for h, ww in enumerate((wr_, wi_)):
                    col = ww[:, :, TP:TP + 1]
                    chain(v.tensor_tensor(col, col, at(INJ + 32 * h, PAIRS)[:, bass.ds(i * QP, QP)].unsqueeze(2), ALU.add))
                for h in range(2):
                    v.tensor_tensor_scan(flat(XRI + h * QP * N), flat(DEC), flat(W + h * QP * N), 0.0, ALU.mult, ALU.add)\
                        .then_inc(sem("dve_chain"), 1)
                    chain.n += 1
                dve.wait_ge(sem("dve_chain"), chain.turn + chain.n)
                turn(wr_, xr, er, xi, ei, ALU.subtract)
                turn(wi_, xi, er, xr, ei, ALU.add)
                for h, ww in enumerate((wr_, wi_)):
                    ins = v.tensor_scalar(fin[:, :, h, bass.ds(i * QP, QP)], ww[:, :, TP - 1:N:TS].rearrange("p q t -> p t q"),
                                          1.0, None, ALU.mult)
                    ins.then_inc(sem("h_ready" if h else "dve_chain"), 1)
                chain.n += 1
                dve.wait_ge(sem("h_ready"), i + 1)
                src = vp[:, bass.ds(i, 1), :]
                a1 = acc.unsqueeze(1)

                def wk(k):
                    return cv[:, bass.ds(i + (c_cw + k * KC), 1)]

                v.memset(at(PAR + 3, 1), 0.0).then_inc(sem("rot_done"), 1)
                sums = (a1, at(ACC2, CW).unsqueeze(1))

                def step(ins):
                    ins.then_inc(sem("dve_chain"), 1)
                    chain.n += 1

                step(v.tensor_scalar(sums[0], src[:, :, 0:CW], wk(0), cv[:, bass.ds(i + c_cb, 1)], ALU.mult, ALU.add))
                step(v.tensor_scalar(sums[1], src[:, :, 1:1 + CW], wk(1), None, ALU.mult))
                for k in range(2, TAPS):
                    if k == 20:
                        dve.wait_ge(sem("c_done"), 1 + i + 1)
                        v.scalar_tensor_tensor(ut[:, bass.ds(i, 1), :], ut[:, bass.ds(i, 1), :],
                                               cv[:, bass.ds(i + c_ds, 1)], pb[:, 6:7, 0:N], ALU.mult, ALU.add)\
                            .then_inc(sem("ys_done"), 1)
                    dve.wait_ge(sem("dve_chain"), chain.turn + (chain.n - 1))
                    s_ = sums[k % 2]
                    step(v.scalar_tensor_tensor(s_, src[:, :, k:k + CW], wk(k), s_, ALU.mult, ALU.add))
                dve.wait_ge(sem("dve_chain"), chain.turn + chain.n)
                v.tensor_tensor(vp[:, bass.ds(i, 1), 0:CW], sums[0], sums[1], ALU.add).then_inc(sem("conv_done"), 1)
            chain.leave(KC)

            sb = at(SBT2, 4, N)
            dve.wait_ge(sem("g_out"), 1 + 16)

            def glu_products(q):
                dve.wait_ge(sem("block_done2"), glu_fill[0] + q + 1)
                dve.wait_ge(sem("glub_out"), 1 + q + 1)
                v.tensor_tensor(sb, pb[:, 0:4, 0:N], sb, ALU.mult).then_inc(sem("glua_out"), 1)
                dve.wait_ge(sem("glua_out"), 1 + q + 1)
                quad = bass.ds(q * 4, 4)
                v.tensor_tensor(mt[:, quad, :], sb, sg[:, quad, :], ALU.mult).then_inc(sem("glu_m"), 1)

            glu_products(0)
            mu, sd, t3, t4 = (at(MU + n * CW, CW) for n in range(4))
            dve.wait_ge(sem("mean_done"), 1)
            v.tensor_scalar(mu, pb[:, 7, 0:CW], 1.0 / DC, None, ALU.mult).then_inc(sem("mu_done"), 1)
            dve.wait_ge(sem("mu_done"), 1)
            dve.wait_ge(sem("conv_done"), KC)
            v.tensor_tensor(vp[:, :, 0:CW], vp[:, :, 0:CW], mu.unsqueeze(1).to_broadcast([P, KC, CW]), ALU.subtract)\
                .then_inc(sem("xc_done"), 1)
            glu_products(1)
            dve.wait_ge(sem("var_done"), 1)
            v.tensor_scalar(mu, pb[:, 4, 0:CW], 1.0 / DC, EPS, ALU.mult, ALU.add).then_inc(sem("var_read"), 1)
            dve.wait_ge(sem("sd_ln"), 1)
            chain(v.reciprocal(sd, sd))
            chain(v.tensor_tensor(t3, sd, sd, ALU.mult))
            chain(v.tensor_tensor(t3, t3, mu, ALU.mult))
            chain(v.tensor_scalar(t3, t3, -0.5, 1.5, ALU.mult, ALU.add))
            chain(v.tensor_tensor(sd, sd, t3, ALU.mult))
            dve.wait_ge(sem("sq_ln"), 1)
            chain(v.tensor_tensor(vp[:, :, 0:CW], vp[:, :, 0:CW], sd.unsqueeze(1).to_broadcast([P, KC, CW]), ALU.mult))
            for c in range(KC):
                chain(v.tensor_scalar(vp[:, c, 0:CW], vp[:, c, 0:CW], cv[:, c_lg + c:c_lg + c + 1],
                                      cv[:, c_lb + c:c_lb + c + 1], ALU.mult, ALU.add))
            v.memset(at(PAR + 4, 1), 0.0).then_inc(sem("z_done"), 1)
            dve.wait_ge(sem("z_sig"), 1)
            yb, sq = at(YB, KC, N), at(SQ, KC, CW)
            v.tensor_tensor(yb[:, :, 0:TP], vp[:, :, 0:TP], sq[:, :, 0:TP], ALU.mult)
            v.tensor_tensor(yb[:, :, TP:N], vp[:, :, SMP:CW], sq[:, :, SMP:CW], ALU.mult).then_inc(sem("yb_done"), 1)
            with dve.Fori(2, 4) as i:
                glu_products(i)
            dve.wait_ge(sem("glu_m"), 1 + 4)
            with dve.Fori(0, 2) as i:
                chain.enter(i, 2)
                for t in range(2):
                    q = bass.ds(i * 8 + 4 * t, 4)
                    qb = bass.ds(i * 8 + 4 * t + KD, 4)
                    dve.wait_ge(sem(f"block_done{1 + t}"), co_fill[t] + i + 1)
                    v.tensor_tensor(sb, pb[:, 4 * t:4 * t + 4, 0:N], sg[:, qb, :], ALU.mult).then_inc(sem(f"co_out{t}"), 1)
                    dve.wait_ge(sem(f"co_out{t}"), 1 + i + 1)
                    chain(v.tensor_tensor(mt[:, q, :], mt[:, q, :], sb, ALU.add))
            chain.leave(2)
            v.memset(at(PAR + 4, 1), 0.0).then_inc(sem("m_done"), 1)
            dve.wait_ge(sem("ht_in"), 16)
            with dve.Fori(0, 4) as i:
                for t in range(2):
                    q = bass.ds(i * 4 + 2 * t, 2)
                    dve.wait_ge(sem(f"block_done{t}"), wo_fill[t] + i + 1)
                    v.tensor_tensor(ht[:, q, :], pb[:, 2 * t:2 * t + 2, 0:N], ht[:, q, :], ALU.add)\
                        .then_inc(sem(f"wo_out{t}"), 1)
            dve.wait_ge(sem("ms2"), 1)
            r = root(pb[:, 4, 0:N], N, [at(RT + n * N, N) for n in range(3)], 1.0 / D, sem("v2"), (sem("sd2"), 1))
            for k in range(KD):
                v.scalar_tensor_tensor(xn[:, k, :], ht[:, k, :], cv[:, c_ffn + k:c_ffn + k + 1], r, ALU.mult, ALU.mult)\
                    .then_inc(sem("xn2_ready"), 1)

            def rt(off, *shape):
                return at(RT + off, *shape, rows=TOK)

            def bc(x, n):
                return x.unsqueeze(2).to_broadcast([TOK, NT, n])

            dve.wait_ge(sem("xn2_ready"), KD)
            rev, iot = at(REV, EXPERTS, rows=TOK), at(IOT, SLOTS, rows=TOK)
            chain(v.tensor_copy(rev, rev.bitcast(I32)))
            dve.wait_ge(sem("iota_done"), 1)
            chain(v.tensor_copy(iot, iot.bitcast(I32)))
            lg, gl = rt(0, NT, 36), rt(108, NT, EG)
            ex, gm, eq4, wm = rt(120, NT, EG), rt(132, NT), rt(136, NT, EG), rt(148, NT)
            dif, ed, pg, w1, w2, v1, v2 = (rt(o, NT) for o in (153, 156, 160, 164, 168, 172, 176))
            lm, o1, o2, eq, a = (rt(180 + 0, NT, 32), rt(276, NT, 32), rt(372, NT, 32), rt(468, NT, 32), rt(600, NT, 32))
            msk, sl, off, incl, one32 = rt(700, NT, 32), rt(800, NT, 32), at(RT + 900, 32), at(RT + 932, 32), at(RT + 964, 32)

            def best(x, n, m, e, onehot):
                chain(v.tensor_reduce(m, x, AX, ALU.max))
                chain(v.tensor_tensor(e, x, bc(m, n), ALU.is_equal))
                chain(v.tensor_tensor(e, e, rev[:, 0:n].unsqueeze(1).to_broadcast([TOK, NT, n]), ALU.mult))
                chain(v.tensor_reduce(wm, e, AX, ALU.max))
                chain(v.tensor_tensor(onehot, e, bc(wm, n), ALU.is_equal))

            dve.wait_ge(sem("logits"), 1)
            dve.wait_ge(sem("wr_in"), 64)
            chain(v.tensor_tensor(lg, pb[0:TOK, 5, 0:108].rearrange("p (j c) -> p j c", c=36),
                                  at(RB, 36, rows=TOK).unsqueeze(1).to_broadcast([TOK, NT, 36]), ALU.add))
            best(lg[:, :, 0:EG], EG, gm, eq4, eq4)
            v.tensor_tensor(gl, lg[:, :, 0:EG], bc(gm, EG), ALU.subtract).then_inc(sem("rt_g"), 1)
            chain(v.tensor_copy(msk.rearrange("p j (g e) -> p j g e", e=EPG), eq4.unsqueeze(3).to_broadcast([TOK, NT, EG, EPG])))
            chain(v.tensor_tensor(lm, lg[:, :, EG:36], msk, ALU.mult))
            chain(v.tensor_scalar(msk, msk, 1e30, 1e30, ALU.mult, ALU.subtract))
            chain(v.tensor_tensor(lm, lm, msk, ALU.add))
            best(lm, 32, v1, eq, o1)
            chain(v.scalar_tensor_tensor(lm, o1, -3e38, lm, ALU.mult, ALU.add))
            best(lm, 32, v2, eq, o2)
            v.tensor_tensor(dif, v2, v1, ALU.subtract).then_inc(sem("rt_d"), 1)
            v.tensor_tensor(a, o1, o2, ALU.add).then_inc(sem("assigned"), 1)
            dve.wait_ge(sem("rt_ge"), 1)
            chain(v.tensor_reduce(pg, ex, AX, ALU.add))
            dve.wait_ge(sem("rt_de"), 1)
            chain(v.tensor_scalar(w1, ed, 1.0, None, ALU.add))
            chain(v.tensor_tensor(w1, w1, pg, ALU.mult))
            chain(v.reciprocal(w1, w1))
            chain(v.tensor_tensor(w2, w1, ed, ALU.mult))
            chain(v.memset(one32, 1.0))
            dve.wait_ge(sem("ranks"), 1)
            chain(v.tensor_tensor_scan(incl, one32, pb[:, 3, 0:32], 0.0, ALU.mult, ALU.add))
            chain(v.tensor_tensor(off, incl, pb[:, 3, 0:32], ALU.subtract))
            v.tensor_copy(at(CNTI, 32, rows=1).bitcast(I32), pb[0:1, 3, 0:32])
            chain(v.tensor_copy(at(OFFI, 32, rows=1).bitcast(I32), at(RT + 900, 32, rows=1)))
            v.memset(at(PAR + 4, 1), 0.0).then_inc(sem("route_ints"), 1)
            chain(v.tensor_tensor(sl, pb[0:TOK, 2, 0:96].rearrange("p (j c) -> p j c", c=32),
                                  at(RT + 900, 32, rows=TOK).unsqueeze(1).to_broadcast([TOK, NT, 32]), ALU.add))
            sf = at(S1F, 2, NT, rows=TOK)
            for n, o in enumerate((o1, o2)):
                chain(v.tensor_tensor(eq, o, sl, ALU.mult))
                chain(v.tensor_reduce(sf[:, n, :], eq, AX, ALU.add))
            chain(v.tensor_copy(at(IDX, 2, NT, rows=TOK).bitcast(I32), sf))
            oh, gw, tmp = (at(x, NT, SLOTS, rows=TOK) for x in (OH, GW, TMP))
            for j in range(NT):
                chain(v.tensor_scalar(tmp[:, j, :], iot, sf[:, 0, j:j + 1], None, ALU.is_equal))
                chain(v.scalar_tensor_tensor(oh[:, j, :], iot, sf[:, 1, j:j + 1], tmp[:, j, :], ALU.is_equal, ALU.add))
            v.memset(at(PAR + 4, 1), 0.0).then_inc(sem("onehot"), 1)
            for j in range(NT):
                chain(v.tensor_scalar(tmp[:, j, :], iot, sf[:, 0, j:j + 1], w1[:, j:j + 1], ALU.is_equal, ALU.mult))
                chain(v.tensor_scalar(gw[:, j, :], iot, sf[:, 1, j:j + 1], w2[:, j:j + 1], ALU.is_equal, ALU.mult))
                chain(v.tensor_tensor(gw[:, j, :], gw[:, j, :], tmp[:, j, :], ALU.add))
            v.memset(at(PAR + 4, 1), 0.0).then_inc(sem("gateweights"), 1)
            xg = at(XG, KD, XW_COLS)
            for k in range(KD):
                dve.wait_ge(sem("xg_mm1"), k + 1)
                v.tensor_copy(xg[:, k, N:2 * N], pb[:, 5 + 2 * (k % 2), 0:N]).then_inc(sem("xg_dve"), 1)
            v.memset(at(PAR + 4, 1), 0.0).then_inc(sem("route_done"), 1)
            dve.wait_ge(sem("gate_mm"), 1)
            v.tensor_copy(at(GATE + N, N), pb[:, 1, 0:N]).then_inc(sem("gate_rows"), 1)
            dve.wait_ge(sem("gate_rows"), 2)
            dve.wait_ge(sem("xg_pad"), 2)
            y = at(Y, KD, XW_COLS)
            with dve.Fori(0, EXPERTS) as e:
                chain.enter(e, 2)
                n0 = chain.n
                cnt = dve.value_load(at(CNTI, EXPERTS, rows=1).bitcast(I32)[0:1, bass.ds(e, 1)], min_val=0, max_val=N)

                def expert(wide):
                    width = WIDE if wide else NARROW
                    off_e = first_slot(dve, e, wide)
                    chain.n = n0
                    gp = pb[:, 4:6, 0:WIDE] if wide else pb[:, 4, 0:2 * NARROW].rearrange("p (c n) -> p c n", n=NARROW)
                    upp = pb[:, 6:8, 0:WIDE] if wide else pb[:, 5, 0:2 * NARROW].rearrange("p (c n) -> p c n", n=NARROW)
                    s, t, h = (at(HID + 576 * n, 2, WIDE)[:, :, 0:width] for n in range(3))
                    dve.wait_ge(sem("sig_done"), e + 1)
                    chain(v.tensor_tensor(t, gp, s, ALU.mult))
                    chain(v.tensor_tensor(t, t, at(GATE, XW_COLS)[:, bass.ds(off_e, width)].unsqueeze(1).to_broadcast([P, 2, width]), ALU.mult))
                    dve.wait_ge(sem("block_done0"), exp_fill[1] + e + 1)
                    v.tensor_tensor(h, upp, t, ALU.mult).then_inc(sem("hid_done"), 1)
                    if wide:
                        for c in range(8, KD):
                            dve.wait_ge(sem("down_done"), 1 + e * KD + c + 1)
                            v.tensor_scalar(y[:, c, bass.ds(off_e, WIDE)], pb[:, 2 + c % 2, 0:WIDE], 1.0, None, ALU.mult).then_inc(sem("down_dve"), 1)
                    else:
                        dve.wait_ge(sem("down_done"), 1 + e * KD + KD)
                        v.tensor_scalar(y[:, 8:KD, bass.ds(off_e, NARROW)].rearrange("p (b c) n -> p b c n", c=4),
                                        pb[:, 2:4, 0:4 * NARROW].rearrange("p b (c n) -> p b c n", n=NARROW),
                                        1.0, None, ALU.mult).then_inc(sem("down_dve"), 8)

                with dve.If(cnt < NARROW + 1):
                    expert(False)
                with dve.Else():
                    expert(True)
            chain.leave(EXPERTS)

            def row_place(n):
                s, g = divmod(n, 4)
                if s < SLOTS // TOK:
                    return arena[0:TOK, s * D + g * 512:s * D + (g + 1) * 512]
                return arena[0:TOK, HN + (s - SLOTS // TOK) * D + g * 512:HN + (s - SLOTS // TOK) * D + (g + 1) * 512]

            for n in range(1, 4 * (SLOTS // TOK + NT), 2):
                dve.wait_ge(sem("row_t"), n + 1)
                v.tensor_copy(row_place(n), pb[0:TOK, n % 8, :]).then_inc(sem("row_dve"), 1)
            yg = at(YG, NT, 2, D, rows=TOK)
            dve.wait_ge(sem("row_act"), 18)
            dve.wait_ge(sem("row_dve"), 18)
            dve.wait_ge(sem("gf_in"), 16)
            for j in range(NT):
                dve.wait_ge(sem(f"rows_in{j}"), 32)
                chain(v.tensor_tensor(yg[:, j, 0, :], yg[:, j, 0, :], yg[:, j, 1, :], ALU.add))
                v.tensor_tensor(yg[:, j, 0, :], yg[:, j, 0, :], at(HN, NT, D, rows=TOK)[:, j, :], ALU.add)\
                    .then_inc(sem("sum_done"), 1)
                ss, sd_, vv, t_ = (at(RT + 4 * j + n, 1, rows=TOK) for n in (0, 1, 2, 3))
                dve.wait_ge(sem("ss_done"), j + 1)
                v.tensor_scalar(ss, ss, 1.0 / D, EPS, ALU.mult, ALU.add).then_inc(sem("vf"), 1)
                dve.wait_ge(sem("sdf"), j + 1)
                chain(v.reciprocal(sd_, sd_))
                chain(v.tensor_tensor(t_, sd_, sd_, ALU.mult))
                chain(v.tensor_tensor(t_, t_, ss, ALU.mult))
                chain(v.tensor_scalar(t_, t_, -0.5, 1.5, ALU.mult, ALU.add))
                chain(v.tensor_tensor(sd_, sd_, t_, ALU.mult))
                v.scalar_tensor_tensor(yg[:, j, 0, :], yg[:, j, 0, :], sd_, at(GF, D, rows=TOK), ALU.mult, ALU.mult)\
                    .then_inc(sem("y_done"), 1)


_OUTS = {
    "y_prompt": (1, TP, D), "y_sample": (1, TS, D),
    "re_p": (1, 1, G, PS), "im_p": (1, 1, G, PS), "conv_p": (1, 1, PAD, DC),
    "re_s": (1, 1, G, PS), "im_s": (1, 1, G, PS), "conv_s": (1, 1, PAD, DC),
}


def kernel(**inputs):
    import numpy as np
    import concourse.bacc as bacc
    from concourse.bass_utils import run_bass_kernel_spmd as run

    nc = bacc.Bacc("TRN2", target_bir_lowering=False, num_devices=1)
    arrays, ins, outs = {}, {}, {}
    for name, a in inputs.items():
        a = np.ascontiguousarray(a)
        arrays["in_" + name] = a
        ins[name] = nc.dram_tensor("in_" + name, a.shape, mybir.dt.from_np(a.dtype), kind="ExternalInput").ap()
    for name, shape in _OUTS.items():
        outs[name] = nc.dram_tensor("out_" + name, shape, F32, kind="ExternalOutput").ap()
    xt_dram = nc.dram_tensor("xt_keep", (P, KD * N), F32, kind="Internal").ap()
    slots_dram = nc.dram_tensor("slot_rows", (SLOTS, D), F32, kind="Internal").ap()
    build(nc, ins, outs, xt_dram, slots_dram)
    r = run(nc, [arrays], core_ids=[0])
    return tuple(r.results[0]["out_" + name] for name in _OUTS)
```

```python
import math
from contextlib import ExitStack

import concourse.bass as bass
from concourse import mybir
from concourse.alu_op_type import AluOpType as ALU

F32 = mybir.dt.float32
I32 = mybir.dt.int32
F32R = mybir.dt.float32r
ACT = mybir.ActivationFunctionType
AX = mybir.AxisListType.X

P = 128
D = 2048
KD = D // P
DC = 1024
KC = DC // P
TP, TS = 256, 32
N = TP + TS
TOK, NT = 96, N // 96
G, PS, HC = 64, 64, 16
PAIRS = G // 2
QP = 4
TAPS = 31
PAD = TAPS - 1
VW = PAD + TP + PAD + TS
CW = VW - PAD
SMP = PAD + TP
EXPERTS, EG, EPG, FE = 32, 4, 8, 256
SLOTS = 2 * N
ST = -(-SLOTS // P)
NARROW, WIDE = 64, N
XW_COLS = 800
assert SLOTS - (NARROW + 1) + WIDE <= XW_COLS
DOWN_N = 96
EPS = 1e-6
ROUND = 12582912.0
TWO_PI_1 = 6.28125
TWO_PI_2 = float(int((2 * math.pi - TWO_PI_1) * 2 ** 20) / 2 ** 20)
TWO_PI_3 = 2 * math.pi - TWO_PI_1 - TWO_PI_2
SLOT = 4096
RING_SIZE = 3 * SLOT
ARENA_AT = 16512


class Slots:

    def __init__(self):
        self.fills = [0, 0, 0]

    def use(self, slot):
        self.fills[slot] += 1
        return self.fills[slot] - 1

    def loop(self, plan, turns):
        first = [self.fills[s] for s in plan]
        for s in plan:
            self.fills[s] += turns
        assert len(set(plan)) == len(plan)
        return first


class Chain:

    def __init__(self, eng, sem):
        self.eng, self.sem, self.n, self.turn = eng, sem, 0, 0

    def __call__(self, ins):
        self.n += 1
        ins.then_inc(self.sem, 1)
        self.eng.wait_ge(self.sem, self.turn + self.n)

    def enter(self, i, per_turn):
        self.turn, self.start, self.per_turn = i * per_turn, self.n, per_turn

    def leave(self, turns):
        assert self.n - self.start == self.per_turn, self.n - self.start
        self.n = self.start + turns * self.per_turn
        self.turn = 0


def build(nc, i_, o_, xt_dram, h_dram, slots_dram):
    ctx = ExitStack()
    with ctx:
        weights = nc.alloc_sbuf_tensor_at("weights", [P, RING_SIZE], F32, offset=ARENA_AT)
        arena = nc.alloc_sbuf_tensor_at("arena", [P, 53000 - RING_SIZE], F32, offset=ARENA_AT + 4 * RING_SIZE)
        pb = ctx.enter_context(nc.psum_tensor("pb", [P, 8, 512], F32))
        made = {}

        def sem(name):
            if name not in made:
                made[name] = ctx.enter_context(nc.semaphore(name))
            return made[name]

        def at(off, *shape, rows=P):
            size = math.prod(shape)
            v = weights[0:rows, off:off + size] if off < RING_SIZE else arena[0:rows, off - RING_SIZE:off - RING_SIZE + size]
            if len(shape) == 2:
                v = v.rearrange("p (a b) -> p a b", b=shape[1])
            if len(shape) == 3:
                v = v.rearrange("p (a b c) -> p a b c", b=shape[1], c=shape[2])
            return v

        def stretch(name, off, size, dtype=F32R):
            return nc.alloc_sbuf_tensor_at(name, [P, size], dtype, offset=ARENA_AT + 4 * off)

        RING = [s * SLOT for s in range(3)]
        IDENT, ONES, CV, TRI = 12288, 12416, 12544, 13016
        WR, RB = 13112, 13688
        FO = 13828
        S1F = 14340
        IDX = 14352
        CNTI, OFFI = 14364, 14396
        MAG, INJ = 14428, 14460
        FIN = 14524
        PAR = 14652
        REV = 14660
        XN, SG, UT, VP, ALLW = 14888, 19496, 28712, 31016, 33800
        XRI, E, DEC, W, T = 37896, 40200, 42504, 43656, 45960
        ACC, UCUR, BCUR, CCUR = 47112, 47430, 47718, 47974
        ACC2 = 52326
        EL, SBT = 48230, 50278
        PT = 50278
        XNAT = 37896
        XT = SG
        ROWS, LD, BR, CR, CACHE = 44400, 44912, 44928, 45952, 46976
        SPA = 37896
        BBP, CPAD = 40200, 42248
        VOUT = SG + 4608
        YB, MU = 33800, 36104
        SBT2, SQ, MT, HT = 37896, 39048, 42504, 48392
        WH, UH, YH, MH = XN, HT, HT + KC * N, UT
        w_high_uv, x_high, x_low = stretch("w_high_uv", ALLW, 4096), stretch("x_high", SG + KD * N, KD * N), stretch("x_low", XT, KD * N)
        V_AT, GLU_AT, CO_AT, WO_AT = 4, 12, 20, 24
        u_full, y_full, m_full = stretch("u_full", UT, KC * N, F32), stretch("y_full", YB, KC * N, F32), stretch("m_full", MT, KD * N, F32)
        w_high, w_low = stretch("w_high", WH, 4096), stretch("w_low", 0, 3 * SLOT)
        u_high, u_low = stretch("u_high", UH, KC * N), stretch("u_low", UT, KC * N)
        y_high, y_low = stretch("y_high", YH, KC * N), stretch("y_low", YB, KC * N)
        m_high, m_low = stretch("m_high", MH, KD * N), stretch("m_low", MT, KD * N)
        HROWS = 30824
        XNT, OH, TMP, LGT, XG, Y = 46856, 27688, 29416, 30400, 30824, 14888
        XW, IOT, HIDT, HID, RT = 43624, 44424, 44648, 44840, 45800
        GW_T = 14358
        HN, GF, YG = 46856, 27688, 14888

        ident, ones, tri = at(IDENT, P), at(ONES, P), at(TRI, TOK, rows=TOK)
        cv = at(CV, 472)
        c_mix, c_ffn, c_cb, c_lg, c_lb, c_ds = 0, 16, 32, 40, 48, 56
        c_lr, c_li, c_dt, c_sr, c_si, c_cw = 64, 96, 128, 160, 192, 224
        xn, xt, ht = at(XN, KD, N), at(XT, KD, N), at(HT, KD, N)
        sg, ut, vp = at(SG, 2 * KD, N), at(UT, KC, N), at(VP, KC, VW)
        ring = [at(r, SLOT) for r in RING]

        block = ctx.enter_context(nc.Block())
        w_in = i_["w_in"][0]

        def cols(w, c0, width):
            return w[:, bass.ds(c0, width)].rearrange("(k p) c -> p k c", p=P)

        def slot_view(s, width):
            return ring[s].rearrange("p (k c) -> p k c", c=width)

        U_PLAN = [0, 1, 2, 0]
        V_PLAN, G_PLAN, GLU_PLAN, CO_PLAN, WO_PLAN, EXP_PLAN = [2, 1], [0, 1], [2, 0], [1, 2], [0, 1], [2, 0, 1]
        plan = Slots()
        u_fill = [plan.use(s) for s in U_PLAN]
        v_fill = plan.loop(V_PLAN, 4)
        g_fill = plan.loop(G_PLAN, 8)
        glu_fill = plan.loop(GLU_PLAN, 4)
        co_fill = plan.loop(CO_PLAN, 2)
        wo_fill = plan.loop(WO_PLAN, 4)
        exp_fill = plan.loop(EXP_PLAN, EXPERTS)
        FIRST = {
            "pe": ("x_done0", "x_done1", "c_done", "down_done"),
            "act": ("vb_out", "x_out0", "x_out1", "g_out", "glub_out", "down_act"),
            "dve": ("v_done", "rot_done", "ys_done", "glua_out", "glu_m", "co_out0", "co_out1", "wo_out0", "wo_out1",
                    "down_dve"),
        }

        def first_slot(eng, e, wide):
            return eng.value_load(at(OFFI, EXPERTS, rows=1).bitcast(I32)[0:1, bass.ds(e, 1)], min_val=0,
                                  max_val=SLOTS - (NARROW + 1) if wide else SLOTS)

        @block.sync
        def _(sp):
            slots = Slots()

            def load(s, fill, src, width):
                sp.wait_ge(sem(f"block_done{s}"), fill)
                sp.dma_start(slot_view(s, width), src).then_inc(sem(f"slot_full{s}"), 16)

            x_p, x_s = i_["x_prompt"][0], i_["x_sample"][0]
            nat = at(XNAT, NT, D, rows=TOK)
            sp.dma_start(nat[:, 0, :], x_p[0:96, :]).then_inc(sem("x_in"), 16)
            sp.dma_start(nat[:, 1, :], x_p[96:192, :]).then_inc(sem("x_in"), 16)
            sp.dma_start(nat[0:64, 2, :], x_p[192:256, :]).then_inc(sem("x_in"), 16)
            sp.dma_start(nat[64:96, 2, :], x_s[:, :]).then_inc(sem("x_in"), 16)
            for b, s in enumerate(U_PLAN[:3]):
                load(s, slots.use(s), cols(w_in, b * 256, 256), 256)
            sp.wait_ge(sem("xt_act"), 4)
            sp.wait_ge(sem("xt_dve"), 4)
            sp.dma_start(xt_dram, at(XT, KD * N)).then_inc(sem("xt_out"), 16)
            load(0, slots.use(0), cols(w_in, 3 * 256, 256), 256)
            f = slots.loop([2, 1], 4)
            with sp.Fori(0, 4) as i:
                load(2, f[0] + i, cols(w_in, i * 256 + 2 * DC, 256), 256)
                load(1, f[1] + i, cols(w_in, i * 256 + DC, 256), 256)
            f = slots.loop([0, 1], 8)
            with sp.Fori(0, 8) as i:
                load(0, f[0] + i, cols(w_in, i * 512 + 3 * DC, 256), 256)
                load(1, f[1] + i, cols(w_in, i * 512 + 3 * DC + 256, 256), 256)
            glu = i_["w_ssm_glu"][0]
            f = slots.loop([2, 0], 4)
            for i in range(4):
                load(2, f[0] + i, cols(glu, i * 512 + D, 512), 512)
                load(0, f[1] + i, cols(glu, i * 512, 512), 512)
            wco = i_["w_conv_out"][0]
            f = slots.loop([1, 2], 2)
            with sp.Fori(0, 2) as i:
                load(1, f[0] + i, cols(wco, i * 1024, 512), 512)
                load(2, f[1] + i, cols(wco, i * 1024 + 512, 512), 512)
            wo = i_["w_out"][0]
            f = slots.loop([0, 1], 4)
            load(0, f[0], cols(wo, 0, 256), 256)
            load(1, f[1], cols(wo, 256, 256), 256)
            sp.wait_ge(sem("co_out1"), 1 + 2)
            sp.dma_start(at(HT, KD * N), xt_dram).then_inc(sem("ht_in"), 16)
            with sp.Fori(0, 3) as i:
                load(0, i + (f[0] + 1), cols(wo, i * 512 + 512, 256), 256)
                load(1, i + (f[1] + 1), cols(wo, i * 512 + 768, 256), 256)
            gate, up, down = i_["w_exp_gate"][0], i_["w_exp_up"][0], i_["w_exp_down"][0]
            f = slots.loop([2, 0, 1], EXPERTS)
            sp.wait_ge(sem("block_done1"), exp_fill[2])
            with sp.Fori(0, EXPERTS) as e:
                load(2, f[0] + e, gate[bass.ds(e, 1)].rearrange("e (p k) c -> p (e k) c", p=P), FE)
                load(0, f[1] + e, up[bass.ds(e, 1)].rearrange("e (p k) c -> p (e k) c", p=P), FE)
                sp.wait_ge(sem("down_done"), 1 + e * KD)
                sp.dma_start(slot_view(1, D), down[bass.ds(e, 1)].rearrange("e (p k) c -> p (e k) c", p=P)).then_inc(sem("slot_full1"), 16)
            sp.wait_ge(sem("h_out"), 48)
            sp.wait_ge(sem("xg_mm1"), KD)
            sp.dma_start(at(HN, NT, D, rows=TOK), h_dram.rearrange("(j p) c -> p j c", p=TOK)).then_inc(sem("h_back"), 16)
            for s in range(ST):
                n = min(P, SLOTS - s * P)
                sp.wait_ge(sem("row_act"), 2 * (s + 1))
                sp.wait_ge(sem("row_dve"), 2 * (s + 1))
                sp.dma_start(slots_dram[s * P:s * P + n, :], at(s * D, D, rows=n)).then_inc(sem("slots_out"), 16)
            o = at(YG, NT, 2, D, rows=TOK)
            for j in range(NT):
                sp.wait_ge(sem("y_done"), j + 1)
                if j < 2:
                    sp.dma_start(o_["y_prompt"][0, j * TOK:(j + 1) * TOK, :], o[:, j, 0, :]).then_inc(sem("out_sp"), 16)
                else:
                    sp.dma_start(o_["y_prompt"][0, 192:256, :], o[0:64, j, 0, :]).then_inc(sem("out_sp"), 16)
                    sp.dma_start(o_["y_sample"][0], o[64:96, j, 0, :]).then_inc(sem("out_sp"), 16)
            sp.wait_ge(sem("out_sp"), 64)

        @block.gpsimd
        def _(po):
            chain = Chain(po, sem("po_chain"))
            po.memset(ident, 0.0).then_inc(sem("po_chain"), 1)
            po.memset(tri, 1.0).then_inc(sem("po_chain"), 1)
            po.memset(ones, 1.0).then_inc(sem("consts"), 1)
            chain.n += 2
            po.wait_ge(sem("po_chain"), 2)
            po.affine_select(out=ident, in_=ident, compare_op=ALU.not_equal, fill=1.0, base=0,
                             pattern=[[-1, P]], channel_multiplier=1).then_inc(sem("consts"), 1)
            po.affine_select(out=tri, in_=tri, compare_op=ALU.is_gt, fill=0.0, base=0,
                             pattern=[[1, TOK]], channel_multiplier=-1).then_inc(sem("consts"), 1)
            po.iota(at(REV, EXPERTS).bitcast(I32), pattern=[[-1, EXPERTS]], base=EXPERTS,
                    channel_multiplier=0).then_inc(sem("consts"), 1)
            po.iota(at(PAR, 1).bitcast(I32), pattern=[[0, 1]], base=0,
                    channel_multiplier=1).then_inc(sem("consts"), 1)
            po.memset(vp[:, :, 0:PAD], 0.0).then_inc(sem("vp_pad"), 1)

            def low_half(wh, s, half, n):
                po.wait_ge(sem("w_high"), n + 1)
                o = s * SLOT + half * 2048
                po.tensor_tensor(w_low[:, o:o + 2048], weights[:, o:o + 2048], wh[:, half * 2048:(half + 1) * 2048], ALU.subtract)\
                    .then_inc(sem("w_low"), 1)

            def low(wh, s, block):
                for half in range(2):
                    low_half(wh, s, half, 2 * block + half)

            low_half(w_high_uv, U_PLAN[0], 0, 0)
            po.wait_ge(sem("xt_out"), 16)
            for g in range(4):
                po.wait_ge(sem("x_high"), g + 1)
                part = slice(g * 4 * N, (g + 1) * 4 * N)
                po.tensor_tensor(x_low[:, part], at(XN, KD * N)[:, part], x_high[:, part], ALU.subtract).then_inc(sem("x_low"), 1)
            low_half(w_high_uv, U_PLAN[0], 1, 1)
            for b in range(1, 4):
                low(w_high_uv, U_PLAN[b], b)
            with po.Fori(0, 4) as i:
                for t in range(2):
                    low(w_high_uv, V_PLAN[t], i * 2 + (V_AT + t))
            po.wait_ge(sem("v_done"), 1 + 4)
            po.wait_ge(sem("prep_done"), 1)
            dec = at(DEC, QP, N)
            chain(po.memset(dec, 0.0))
            elr, eli = at(EL, PAIRS, 16), at(EL + 512, PAIRS, 16)
            ehr, ehi = at(EL + 1024, PAIRS, 16), at(EL + 1536, PAIRS, 16)
            er, ei = at(E, QP, N), at(E + QP * N, QP, N)
            pt, pt2 = at(PT, QP, 16, 16), at(PT + 1024, QP, 16, 16)
            er4 = er[:, :, 0:TP].rearrange("p q (a b) -> p q a b", b=16)
            ei4 = ei[:, :, 0:TP].rearrange("p q (a b) -> p q a b", b=16)
            po.wait_ge(sem("w_free"), 1)
            with po.Fori(0, KC) as i:
                chain.enter(i, 4)
                hi = [t[:, bass.ds(i * QP, QP), :].unsqueeze(3).to_broadcast([P, QP, 16, 16]) for t in (ehr, ehi)]
                lo = [t[:, bass.ds(i * QP, QP), :].unsqueeze(2).to_broadcast([P, QP, 16, 16]) for t in (elr, eli)]
                po.wait_ge(sem("rot_done"), 1 + i)
                po.tensor_tensor(er4, hi[0], lo[0], ALU.mult)
                po.tensor_tensor(pt, hi[1], lo[1], ALU.mult).then_inc(sem("po_chain"), 1)
                po.tensor_tensor(ei4, hi[0], lo[1], ALU.mult)
                po.tensor_tensor(pt2, hi[1], lo[0], ALU.mult).then_inc(sem("po_chain"), 1)
                chain.n += 2
                po.wait_ge(sem("po_chain"), chain.turn + chain.n)
                po.tensor_tensor(er4, er4, pt, ALU.subtract).then_inc(sem("po_chain"), 1)
                po.tensor_tensor(ei4, ei4, pt2, ALU.add).then_inc(sem("po_chain"), 1)
                chain.n += 2
                po.wait_ge(sem("po_chain"), chain.turn + chain.n)
                one = ones[:, 0:TS].unsqueeze(1).to_broadcast([P, QP, TS])
                po.tensor_tensor(er[:, :, TP:N], er[:, :, 0:TS], one, ALU.mult).then_inc(sem("tab_ready"), 1)
                po.tensor_tensor(ei[:, :, TP:N], ei[:, :, 0:TS], one, ALU.mult).then_inc(sem("tab_ready"), 1)
                mag = at(MAG, PAIRS)[:, bass.ds(i * QP, QP)].unsqueeze(2)
                po.tensor_copy(dec[:, :, 1:TP], mag.to_broadcast([P, QP, TP - 1])).then_inc(sem("tab_ready"), 1)
                po.tensor_copy(dec[:, :, TP + 1:N], mag.to_broadcast([P, QP, TS - 1])).then_inc(sem("tab_ready"), 1)
            chain.leave(KC)

            low_half(w_high, GLU_PLAN[0], 0, 2 * GLU_AT)
            for half in range(2):
                po.wait_ge(sem("u_high"), half + 1)
                part = slice(half * 4 * N, (half + 1) * 4 * N)
                po.tensor_tensor(u_low[:, part], u_full[:, part], u_high[:, part], ALU.subtract).then_inc(sem("u_low"), 1)
            low_half(w_high, GLU_PLAN[0], 1, 2 * GLU_AT + 1)
            low(w_high, GLU_PLAN[1], GLU_AT + 1)
            for first, turns, slots_ in ((GLU_AT + 2, 3, GLU_PLAN), (CO_AT, 2, CO_PLAN), (WO_AT, 4, WO_PLAN)):
                with po.Fori(0, turns) as i:
                    for t in range(2):
                        low(w_high, slots_[t], i * 2 + (first + t))

            po.wait_ge(sem("block_done1"), wo_fill[1] + 4)
            po.iota(at(IOT, SLOTS, rows=TOK).bitcast(I32), pattern=[[1, SLOTS]], base=0,
                    channel_multiplier=0).then_inc(sem("iota_done"), 1)
            xg = at(XG, KD, XW_COLS)
            po.wait_ge(sem("h_out"), 48)
            po.memset(xg[:, :, SLOTS:XW_COLS], 0.0).then_inc(sem("xg_pad"), 1)
            po.wait_ge(sem("route_ints"), 1)

            def window(e):
                off = po.value_load(at(OFFI, EXPERTS, rows=1).bitcast(I32)[0:1, bass.ds(e, 1)],
                                    min_val=0, max_val=SLOTS)
                po.wait_ge(sem("block_done0"), exp_fill[1] + e)
                po.tensor_copy(at(XW, KD, NARROW), xg[:, :, bass.ds(off, NARROW)]).then_inc(sem("xw_ready"), 1)

            po.wait_ge(sem("xg_act"), KD)
            with po.Fori(0, 1) as e:
                window(e)
            po.wait_ge(sem("xg_dve"), KD)
            with po.Fori(1, EXPERTS) as e:
                window(e)

            po.wait_ge(sem("slots_out"), 16 * ST)
            idx = at(IDX, 2, NT, rows=TOK).bitcast(I32)
            yg = at(YG, NT, 2, D, rows=TOK)
            for j in range(NT):
                for r in range(2):
                    po.indirect_dma_start(
                        out=yg[:, j, r, :], out_offset=None, in_=slots_dram[:, :],
                        in_offset=bass.IndirectOffsetOnAxis(ap=idx[:, r, j:j + 1], axis=0),
                    ).then_inc(sem(f"rows_in{j}"), 16)
            po.wait_ge(sem("gf_in"), 16)
            for j in range(NT):
                po.wait_ge(sem("sum_done"), j + 1)
                po.tensor_tensor(yg[:, j, 1, :], yg[:, j, 0, :], at(GF, D, rows=TOK), ALU.mult).then_inc(sem("gained"), 1)

        @block.tensor
        def _(pe):
            for name in FIRST["pe"]:
                pe.sem_inc(sem(name), 1)
            slots = Slots()

            def mm(out, lhsT, rhs, first, last):
                return pe.matmul(out, lhsT, rhs, start=first, stop=last)

            def products(s, fill, kt, width, rhs, outs, each=None):
                pe.wait_ge(sem(f"slot_full{s}"), (fill + 1) * 16)
                w = slot_view(s, width)
                for c, out in enumerate(outs):
                    for k in range(kt):
                        last = mm(out, w[:, k, c * P:(c + 1) * P], rhs[:, k, :], k == 0, k == kt - 1)
                last.then_inc(sem(f"block_done{s}"), 1)
                return last

            def split_products(weights_high, s, block, kt, width, high, low, outs, readies=(), per_half=1):
                kh = kt // 2
                wl = w_low[:, s * SLOT:(s + 1) * SLOT].rearrange("p (k c) -> p k c", c=width)
                xh, xl = (t[:, 0:kt * N].rearrange("p (k n) -> p k n", n=N) for t in (high, low))
                for half in range(2):
                    wh = weights_high[:, half * 2048:(half + 1) * 2048].rearrange("p (k c) -> p k c", c=width)
                    ks = range(half * kh, (half + 1) * kh)
                    pe.wait_ge(sem("w_high"), 2 * block + (half + 1))
                    if readies:
                        pe.wait_ge(sem(readies[0]), per_half * (half + 1))
                    for c, out in enumerate(outs):
                        for k in ks:
                            mm(out, wh[:, k - half * kh, c * P:(c + 1) * P], xh[:, k, :], k == 0, False)
                    if readies:
                        pe.wait_ge(sem(readies[1]), per_half * (half + 1))
                    for c, out in enumerate(outs):
                        for k in ks:
                            last = mm(out, wh[:, k - half * kh, c * P:(c + 1) * P], xl[:, k, :], False, False)
                    last.then_inc(sem("w_high_used"), 1)
                    pe.wait_ge(sem("w_low"), 2 * block + (half + 1))
                    for c, out in enumerate(outs):
                        for k in ks:
                            last = mm(out, wl[:, k, c * P:(c + 1) * P], xh[:, k, :], False, k == kt - 1)
                last.then_inc(sem(f"block_done{s}"), 1)

            pe.wait_ge(sem("consts"), 5)
            pe.wait_ge(sem("x_in"), 64)
            nat = at(XNAT, NT * D, rows=TOK).rearrange("p (j k c) -> p j k c", j=NT, c=P)
            for m in range(KD // 2):
                b = 2 * (m % 2)
                if m >= 2:
                    pe.wait_ge(sem("xt_act" if m % 2 == 0 else "xt_dve"), m // 2)
                for kk in range(2):
                    for j in range(NT):
                        last = pe.transpose(pb[:, b + kk, j * TOK:(j + 1) * TOK], nat[:, j, 2 * m + kk, :],
                                            ident[0:TOK, 0:TOK])
                last.then_inc(sem("xt_t"), 1)

            def column_sums(src, bank, kt, width, ready, out, per_wait=1):
                for k in range(kt):
                    if k % per_wait == 0:
                        pe.wait_ge(ready[0], ready[1] + k // per_wait + 1)
                    last = mm(pb[:, bank, 0:width], ones, src[:, k, 0:width], k == 0, k == kt - 1)
                last.then_inc(out, 1)

            column_sums(xn, 5, KD, N, (sem("sq1"), 0), sem("ms1"), per_wait=4)

            pe.wait_ge(sem("rows_in"), 16 * 12)
            pe.wait_ge(sem("dt_rows"), 1)
            o = 0
            for n, r in enumerate((P, TOK, 124, 124)):
                last = pe.transpose(pb[:, 4, o:o + r], at(ROWS + n * P, P, rows=r), ident[0:r, 0:r])
                o += r
            last.then_inc(sem("cv_t"), 1)
            pe.wait_ge(sem("bc_in"), 16 * 5)
            for c in range(KC):
                last = pe.transpose(pb[:, 6, c * PAD:(c + 1) * PAD], at(CACHE, KC, P, rows=PAD)[:, c, :],
                                    ident[0:PAD, 0:PAD])
            last.then_inc(sem("cache_t"), 1)
            for b, s in enumerate(U_PLAN):
                q = 2 * (b % 2)
                if b == 0:
                    pe.wait_ge(sem("xt_act"), 4)
                    pe.wait_ge(sem("xt_dve"), 4)
                if b >= 2:
                    pe.wait_ge(sem("u_out"), b - 1)
                slots.use(s)
                split_products(w_high_uv, s, b, KD, 256, x_high, x_low, [pb[:, q + c, 0:N] for c in range(2)],
                               ("x_high", "x_low") if b == 0 else (), 2)

            slots.loop(V_PLAN, 4)
            pe.wait_ge(sem("u_out"), 4)
            with pe.Fori(0, 4) as i:
                pe.wait_ge(sem("vb_out"), 1 + i)
                split_products(w_high_uv, 2, i * 2 + V_AT, KD, 256, x_high, x_low, [pb[:, 2 + c, 0:N] for c in range(2)])
                pe.wait_ge(sem("v_done"), 1 + i)
                split_products(w_high_uv, 1, i * 2 + (V_AT + 1), KD, 256, x_high, x_low, [pb[:, c, 0:N] for c in range(2)])
            pe.wait_ge(sem("bb_ready"), 1)
            pe.wait_ge(sem("cv_out"), 1)
            pe.wait_ge(sem("cache_out"), 1)
            for c in range(KC):
                b = 4 + c % 4
                if c >= 4:
                    pe.wait_ge(sem("allw_out"), c - 3)
                for h in range(2):
                    pe.transpose(pb[:, b, h * P:(h + 1) * P], at(BBP + h * 1024, KC, P)[:, c, :], ident)
                for h in range(2):
                    last = pe.transpose(pb[:, b, (2 + h) * P:(3 + h) * P], at(CPAD + h * 1024, KC, P)[:, c, :], ident)
                last.then_inc(sem("allw_t"), 1)
            pe.wait_ge(sem("allw_out"), KC)
            pe.wait_ge(sem("v_done"), 1 + 4)
            for g, t0 in enumerate((TP, VW - PAD)):
                for c in range(KC):
                    last = pe.transpose(pb[0:PAD, 4 + 2 * g + c // 4, (c % 4) * P:(c % 4 + 1) * P],
                                        vp[:, c, t0:t0 + PAD], ident)
                last.then_inc(sem("vout_t"), 1)
            pe.wait_ge(sem("vout_copied"), 2)

            f = slots.loop([0, 1], 8)
            h_re, h_im = at(W, QP, N), at(W + QP * N, QP, N)
            with pe.Fori(0, KC) as i:
                pe.wait_ge(sem("cur_ready"), i + 1)
                for q in range(QP):
                    for h in range(2):
                        pe.wait_ge(sem(f"x_out{h}"), 1 + i * QP + q)
                        last = mm(pb[:, 4 + h, 0:N], at(BCUR, 2, P)[32 * q:32 * q + 32, h, :],
                                  at(UCUR, N)[32 * q:32 * q + 32, :], True, True)
                        last.then_inc(sem(f"x_done{h}"), 1)
                for t in range(2):
                    pe.wait_ge(sem("g_out"), 1 + i * 2 + t)
                    products(t, f[t] + i, KD, 256, xn, [pb[:, 2 * t + c, 0:N] for c in range(2)])
                pe.wait_ge(sem("h_ready"), i + 1)
                pe.wait_ge(sem("ccur_ready"), i + 1)
                pe.wait_ge(sem("ys_done"), 1 + i)
                for q in range(QP):
                    mm(pb[32 * q:32 * q + 32, 6, 0:N], at(CCUR, 2, P)[:, 0, 32 * q:32 * q + 32], h_re[:, q, :], True, False)
                    last = mm(pb[32 * q:32 * q + 32, 6, 0:N], at(CCUR, 2, P)[:, 1, 32 * q:32 * q + 32], h_im[:, q, :], False, True)
                last.then_inc(sem("c_done"), 1)

            pe.wait_ge(sem("rot_done"), 1 + KC)
            for n in range(4):
                last = pe.transpose(pb[0:PAIRS, 5, n * P:(n + 1) * P], at(FIN, 4, PAIRS)[:, n, :], ident)
            last.then_inc(sem("fin_t"), 1)
            pe.wait_ge(sem("g_out"), 1 + 16)
            pe.wait_ge(sem("fin_out"), 1)

            def glu_quad(q):
                pe.wait_ge(sem("glub_out"), 1 + q)
                split_products(w_high, 2, q * 2 + GLU_AT, KC, 512, u_high, u_low, [pb[:, 4 + c, 0:N] for c in range(4)], ("u_high", "u_low"))
                pe.wait_ge(sem("glua_out"), 1 + q)
                split_products(w_high, 0, q * 2 + (GLU_AT + 1), KC, 512, u_high, u_low, [pb[:, c, 0:N] for c in range(4)])

            glu_quad(0)
            pe.wait_ge(sem("conv_done"), KC)
            pe.wait_ge(sem("glub_out"), 1 + 1)
            for c in range(KC):
                last = mm(pb[:, 7, 0:CW], ones, vp[:, c, 0:CW], c == 0, c == KC - 1)
            last.then_inc(sem("mean_done"), 1)
            pe.wait_ge(sem("mu_done"), 1)
            glu_quad(1)
            pe.wait_ge(sem("sq_ln"), 1)
            pe.wait_ge(sem("glub_out"), 1 + 2)
            for c in range(KC):
                last = mm(pb[:, 4, 0:CW], ones, at(SQ, KC, CW)[:, c, :], c == 0, c == KC - 1)
            last.then_inc(sem("var_done"), 1)
            pe.wait_ge(sem("var_read"), 1)
            with pe.Fori(2, 4) as i:
                glu_quad(i)
            pe.wait_ge(sem("yb_done"), 1)
            pe.wait_ge(sem("glua_out"), 1 + 4)
            pe.wait_ge(sem("glub_out"), 1 + 4)
            with pe.Fori(0, 2) as i:
                for t in range(2):
                    pe.wait_ge(sem(f"co_out{t}"), 1 + i)
                    split_products(w_high, 1 + t, i * 2 + (CO_AT + t), KC, 512, y_high, y_low, [pb[:, 4 * t + c, 0:N] for c in range(4)])
            pe.wait_ge(sem("co_out0"), 1 + 2)
            pe.wait_ge(sem("co_out1"), 1 + 2)
            with pe.Fori(0, 4) as i:
                for t in range(2):
                    pe.wait_ge(sem(f"wo_out{t}"), 1 + i)
                    split_products(w_high, t, i * 2 + (WO_AT + t), KD, 256, m_high, m_low, [pb[:, 2 * t + c, 0:N] for c in range(2)],
                                   ("m_high", "m_low") if t == 0 else ())
            for plan_, turns in ((GLU_PLAN, 4), (CO_PLAN, 2), (WO_PLAN, 4)):
                slots.loop(plan_, turns)
            column_sums(at(SG, KD, N), 4, KD, N, (sem("sq2"), 0), sem("ms2"), per_wait=4)

            for n in range(NT * 4):
                j, g = divmod(n, 4)
                if n >= 4:
                    pe.wait_ge(sem("hr_out"), n - 3)
                elif n == 0:
                    pe.wait_ge(sem("wo_out0"), 1 + 4)
                    pe.wait_ge(sem("wo_out1"), 1 + 4)
                for c in range(4):
                    last = pe.transpose(pb[0:TOK, n % 4, c * P:(c + 1) * P], ht[:, 4 * g + c, j * TOK:(j + 1) * TOK], ident)
                last.then_inc(sem("hr_t"), 1)
            wr = at(WR, KD, EG + EXPERTS)
            pe.wait_ge(sem("wr_in"), 64)
            for k in range(KD):
                pe.wait_ge(sem("xn2_ready"), k + 1)
                last = mm(pb[0:36, 5, 0:N], wr[:, k, :], xn[:, k, :], k == 0, k == KD - 1)
            last.then_inc(sem("lgt"), 1)
            pe.wait_ge(sem("lgt_out"), 1)
            for j in range(NT):
                last = mm(pb[0:TOK, 6, j * 36:(j + 1) * 36], at(LGT, N, rows=36)[:, j * TOK:(j + 1) * TOK],
                          ident[0:36, 0:36], True, True)
            last.then_inc(sem("logits"), 1)
            for n in range(NT * 4):
                j, g = divmod(n, 4)
                if n >= 4:
                    pe.wait_ge(sem("xnt_act"), n - 3)
                elif n == 0:
                    pe.wait_ge(sem("hr_out"), NT * 4)
                for c in range(4):
                    last = pe.transpose(pb[0:TOK, n % 4, c * P:(c + 1) * P], xn[:, 4 * g + c, j * TOK:(j + 1) * TOK], ident)
                last.then_inc(sem("xnt_t"), 1)
            a = at(RT + 600, NT, EXPERTS, rows=TOK)
            pe.wait_ge(sem("assigned"), 1)
            for j in range(NT):
                for jj in range(j + 1):
                    mm(pb[0:TOK, 7, j * 32:(j + 1) * 32], tri if jj == j else ones[0:TOK, 0:TOK], a[:, jj, :],
                       jj == 0, jj == j)
            for j in range(NT):
                last = mm(pb[:, 7, 128:160], ones[0:TOK, :], a[:, j, :], j == 0, j == NT - 1)
            last.then_inc(sem("ranks"), 1)
            pe.wait_ge(sem("xnt_act"), NT * 4)
            pe.wait_ge(sem("onehot"), 1)
            xnt = at(XNT, NT, D, rows=TOK)

            def gather(h, banks, out):
                for k in range(KD):
                    if k >= 2:
                        pe.wait_ge(out, k - 1)
                    for j in range(NT):
                        last = mm(pb[:, banks[k % 2], 0:N], xnt[:, j, k::KD],
                                  at(OH, NT, SLOTS, rows=TOK)[:, j, h * N:(h + 1) * N], j == 0, j == NT - 1)
                    last.then_inc(sem(f"xg_mm{h}"), 1)

            gather(0, (4, 5), sem("xg_act"))
            f = slots.loop([2, 0, 1], EXPERTS)
            pe.wait_ge(sem("route_ints"), 1)
            pe.wait_ge(sem("xg_act"), KD)
            pe.wait_ge(sem("xg_pad"), 1)

            def expert(e):
                cnt = pe.value_load(at(CNTI, EXPERTS, rows=1).bitcast(I32)[0:1, bass.ds(e, 1)], min_val=0, max_val=N)

                def narrow():
                    pe.wait_ge(sem("xw_ready"), e + 1)
                    for s, bank, fill in ((2, 4, f[0]), (0, 5, f[1])):
                        pe.wait_ge(sem(f"slot_full{s}"), (fill + e) * 16 + 16)
                        w = slot_view(s, FE)
                        for k in range(KD):
                            half = slice(NARROW * (k % 2), NARROW * (k % 2) + NARROW)
                            last = mm(pb[half, bank, 0:FE], at(XW, KD, NARROW)[:, k, :], w[:, k, :], k < 2, k >= KD - 2)
                        last.then_inc(sem(f"block_done{s}"), 1)
                    pe.wait_ge(sem("hid_done"), e + 1)
                    for k in range(2):
                        last = mm(pb[:, 6, k * DOWN_N:(k + 1) * DOWN_N], at(HID + 1024, FE, rows=NARROW)[:, k::2],
                                  ident[0:NARROW, 0:DOWN_N], True, True)
                    last.then_inc(sem("hid_t"), 1)
                    pe.wait_ge(sem("hid_copied"), e + 1)
                    pe.wait_ge(sem("down_act"), 1 + e * 8)
                    pe.wait_ge(sem("down_dve"), 1 + e * 8)
                    pe.wait_ge(sem("slot_full1"), (f[2] + e) * 16 + 16)
                    w = slot_view(1, D)
                    for c in range(KD):
                        out = pb[:, c // 4, (c % 4) * DOWN_N:(c % 4 + 1) * DOWN_N]
                        for k in range(2):
                            last = mm(out, w[:, k, c * P:(c + 1) * P], at(HIDT, 2, DOWN_N)[:, k, :], k == 0, k == 1)
                        if c % 8 == 7:
                            last.then_inc(sem("down_done"), 8)

                def wide():
                    off = first_slot(pe, e, True)
                    hid = at(HID + 1152, 2, WIDE)
                    pe.wait_ge(sem("xw_ready"), e + 1)
                    for s, base, fill in ((2, 4, f[0]), (0, 6, f[1])):
                        pe.wait_ge(sem(f"slot_full{s}"), (fill + e) * 16 + 16)
                        w = slot_view(s, FE)
                        for c in range(2):
                            for k in range(KD):
                                last = mm(pb[:, base + c, 0:WIDE], w[:, k, c::2],
                                          at(XG, KD, XW_COLS)[:, k, bass.ds(off, WIDE)], k == 0, k == KD - 1)
                        last.then_inc(sem(f"block_done{s}"), 1)
                    pe.sem_inc(sem("hid_t"), 1)
                    pe.wait_ge(sem("hid_done"), e + 1)
                    pe.wait_ge(sem("down_act"), 1 + e * 8)
                    pe.wait_ge(sem("down_dve"), 1 + e * 8)
                    pe.wait_ge(sem("slot_full1"), (f[2] + e) * 16 + 16)
                    w = slot_view(1, D)
                    for c in range(KD):
                        out = pb[:, c % 2 if c < 8 else 2 + c % 2, 0:WIDE]
                        if c % 8 >= 2:
                            pe.wait_ge(sem("down_act" if c < 8 else "down_dve"), 1 + e * 8 + c % 8 - 1)
                        for k in range(2):
                            last = mm(out, w[:, k, c * P:(c + 1) * P], hid[:, k, :], k == 0, k == 1)
                        last.then_inc(sem("down_done"), 1)

                with pe.If(cnt < NARROW + 1):
                    narrow()
                with pe.Else():
                    wide()

            with pe.Fori(0, 1) as e:
                expert(e)
            pe.wait_ge(sem("down_act"), 1 + 8)
            pe.wait_ge(sem("down_dve"), 1 + 8)
            gather(1, (6, 7), sem("xg_dve"))
            with pe.Fori(1, EXPERTS) as e:
                expert(e)

            pe.wait_ge(sem("down_act"), 1 + EXPERTS * 8)
            pe.wait_ge(sem("down_dve"), 1 + EXPERTS * 8)
            for n in range(4 * ST):
                s, g = divmod(n, 4)
                width = min(P, SLOTS - s * P)
                if n >= 8:
                    pe.wait_ge(sem("row_act" if n % 2 == 0 else "row_dve"), n // 2 - 3)
                for c in range(4):
                    last = pe.transpose(pb[0:width, n % 8, c * P:(c + 1) * P],
                                        at(Y, KD, XW_COLS)[:, 4 * g + c, s * P:s * P + width], ident)
                last.then_inc(sem("row_t"), 1)

        @block.scalar
        def _(act):
            for name in FIRST["act"]:
                act.sem_inc(sem(name), 1)
            def row(tile, at_row, name, pattern="(r c) -> r c", c=P):
                src = i_[name]
                while len(src.shape) > 1:
                    src = src.rearrange("a b -> (a b)") if len(src.shape) == 2 else src[0] if src.shape[0] == 1 else src.rearrange(
                        "a b c -> (a b c)") if len(src.shape) == 3 else src
                n = src.shape[0] // P
                act.dma_start(at(ROWS + tile * P, P)[at_row:at_row + n, :], src.rearrange("(r c) -> r c", c=P))\
                    .then_inc(sem("rows_in"), 16)

            act.dma_start(at(LD, 2, rows=PAIRS), i_["log_dt"][0].rearrange("(r c) -> r c", c=2)).then_inc(sem("ld_in"), 16)
            row(0, 0, "norm_mix_g")
            row(0, 16, "norm_ffn_g")
            row(0, 32, "conv_b")
            row(0, 40, "conv_ln_g")
            row(0, 48, "conv_ln_b")
            row(0, 56, "d_skip")
            row(0, 64, "lam_re")
            row(0, 96, "lam_im")
            row(1, 32, "state_ssm_re")
            row(1, 64, "state_ssm_im")
            cw = i_["conv_w"][0].rearrange("k (c p) -> (k c) p", p=P)
            for t in range(2):
                act.dma_start(at(ROWS + (2 + t) * P, P, rows=124), cw[124 * t:124 * t + 124, :]).then_inc(sem("rows_in"), 16)
            act.dma_start(at(CACHE, DC, rows=PAD), i_["cache_conv"][0, 0]).then_inc(sem("bc_in"), 16)
            for h, name in enumerate(("b_re", "b_im")):
                act.dma_start(at(BR + 512 * h, PAIRS, HC), i_[name][0].rearrange("(r g) p h -> (g p) r h", g=2))\
                    .then_inc(sem("bc_in"), 16)
            for h, name in enumerate(("c_re", "c_im")):
                act.dma_start(at(CR + 512 * h, KC, PS), i_[name][0].rearrange("(t g) h p -> (g h) t p", g=8))\
                    .then_inc(sem("bc_in"), 16)
            wr = at(WR, KD, EG + EXPERTS)
            act.dma_start(wr[:, :, 0:EG], i_["w_router_group"][0].rearrange("(k p) c -> p k c", p=P)).then_inc(sem("wr_in"), 16)
            act.dma_start(wr[:, :, EG:EG + EXPERTS], i_["w_router_expert"][0].rearrange("(k p) c -> p k c", p=P)).then_inc(sem("wr_in"), 16)
            rb = at(RB, EG + EXPERTS, rows=TOK)
            act.dma_start(rb[:, 0:EG], i_["b_router_group"][0:1, :].to_broadcast([TOK, EG])).then_inc(sem("wr_in"), 16)
            act.dma_start(rb[:, EG:EG + EXPERTS], i_["b_router_expert"][0:1, :].to_broadcast([TOK, EXPERTS])).then_inc(sem("wr_in"), 16)

            for m in range(0, KD // 2, 2):
                act.wait_ge(sem("xt_t"), m + 1)
                act.activation(xt[:, 2 * m:2 * m + 2, :], pb[:, 0:2, 0:N], ACT.Copy).then_inc(sem("xt_act"), 1)

            def squares(src, dst, n_ready, out):
                for g in range(4):
                    n_ready(g)
                    act.activation(dst[:, 4 * g:4 * g + 4, :], src[:, 4 * g:4 * g + 4, :], ACT.Square).then_inc(out, 1)

            def xt_ready(g):
                act.wait_ge(sem("xt_act"), g + 1)
                act.wait_ge(sem("xt_dve"), g + 1)

            squares(xt, xn, xt_ready, sem("sq1"))

            def high_half(wh, s, fill, half, n):
                act.wait_ge(sem(f"slot_full{s}"), (fill + 1) * 16)
                if not (isinstance(n, int) and n < 2):
                    act.wait_ge(sem("w_high_used"), n - 1)
                    act.wait_ge(sem("w_low"), n - 1)
                act.activation(wh[:, half * 2048:(half + 1) * 2048], weights[:, s * SLOT + half * 2048:s * SLOT + (half + 1) * 2048], ACT.Copy)\
                    .then_inc(sem("w_high"), 1)

            def high(wh, s, fill, block):
                for half in range(2):
                    high_half(wh, s, fill, half, 2 * block + half)

            high(w_high_uv, U_PLAN[0], u_fill[0], 0)
            act.wait_ge(sem("v1"), 1)
            act.activation(at(SBT + N, N), at(SBT, N), ACT.Sqrt).then_inc(sem("sd1"), 1)
            act.wait_ge(sem("cv_t"), 1)
            act.activation(cv, pb[:, 4, 0:472], ACT.Copy).then_inc(sem("cv_out"), 1)
            act.wait_ge(sem("cache_t"), 1)
            act.activation(vp[:, :, PAD + TP:2 * PAD + TP], pb[:, 6, 0:KC * PAD].rearrange("p (c t) -> p c t", t=PAD),
                           ACT.Copy).then_inc(sem("cache_out"), 1)
            act.wait_ge(sem("cv_out"), 1)
            act.activation(at(SPA, 32), cv[:, c_dt:c_dt + 32], ACT.Exp).then_inc(sem("dt_exp"), 1)
            for g in range(4):
                act.wait_ge(sem("xn_ready"), 4 * (g + 1))
                part = slice(g * 4 * N, (g + 1) * 4 * N)
                act.activation(x_high[:, part], at(XN, KD * N)[:, part], ACT.Copy).then_inc(sem("x_high"), 1)
            act.wait_ge(sem("lrdt"), 1)
            act.activation(at(MAG, 32), at(SPA + 32, 32), ACT.Exp).then_inc(sem("mag"), 1)
            act.wait_ge(sem("angles"), 1)
            act.activation(at(SPA + 768, 256), at(SPA + 512, 256), ACT.Sin).then_inc(sem("sines"), 1)
            act.activation(at(SPA + 1024, 256), at(SPA + 512, 256), ACT.Sin, scale=0.5).then_inc(sem("sines"), 1)
            for b in range(4):
                if b < 3:
                    high(w_high_uv, U_PLAN[b + 1], u_fill[b + 1], b + 1)
                else:
                    high(w_high_uv, V_PLAN[0], v_fill[0], V_AT)
                act.wait_ge(sem(f"block_done{U_PLAN[b]}"), u_fill[b] + 1)
                act.activation(ut[:, 2 * b:2 * b + 2, :], pb[:, 2 * (b % 2):2 * (b % 2) + 2, 0:N], ACT.Copy)\
                    .then_inc(sem("u_out"), 1)
            def v_gates(i):
                high(w_high_uv, V_PLAN[1], v_fill[1] + i, i * 2 + (V_AT + 1))
                act.wait_ge(sem("block_done2"), v_fill[0] + i + 1)
                act.wait_ge(sem("v_done"), 1 + i)
                act.activation(at(SBT, 2, N), pb[:, 2:4, 0:N], ACT.Sigmoid).then_inc(sem("vb_out"), 1)

            with act.Fori(0, 3) as i:
                v_gates(i)
                high(w_high_uv, V_PLAN[0], v_fill[0] + 1 + i, i * 2 + (V_AT + 2))
            v_gates(3)
            for c in range(KC):
                act.wait_ge(sem("allw_t"), c + 1)
                act.activation(at(ALLW, KC, 512)[:, c, :], pb[:, 4 + c % 4, :], ACT.Copy).then_inc(sem("allw_out"), 1)
            act.wait_ge(sem("xt_out"), 16)
            for g in range(2):
                act.wait_ge(sem("vout_t"), g + 1)
                act.activation(at(VOUT + g * DC, DC, rows=PAD).rearrange("p (a b) -> p a b", b=512),
                               pb[0:PAD, 4 + 2 * g:6 + 2 * g, :], ACT.Copy).then_inc(sem("vout_copied"), 1)
            act.wait_ge(sem("vout_copied"), 2)
            act.dma_start(o_["conv_p"][0, 0], at(VOUT, DC, rows=PAD)).then_inc(sem("vout"), 16)
            act.dma_start(o_["conv_s"][0, 0], at(VOUT + DC, DC, rows=PAD)).then_inc(sem("vout"), 16)
            act.wait_ge(sem("vout"), 32)
            act.wait_ge(sem("w_free"), 1)
            act.wait_ge(sem("allw_out"), KC)
            xr, xi = at(XRI, QP, N), at(XRI + QP * N, QP, N)
            with act.Fori(0, KC) as i:
                act.wait_ge(sem("x_done0"), 1 + i * QP)
                act.wait_ge(sem("x_done1"), 1 + i * QP)
                act.activation(at(UCUR, N), ut[:, bass.ds(i, 1), :], ACT.Copy)
                act.activation(at(BCUR, 256), at(ALLW, KC, 512)[:, bass.ds(i, 1), 0:256], ACT.Copy).then_inc(sem("cur_ready"), 1)
                act.wait_ge(sem("rot_done"), 1 + i)
                for q in range(QP):
                    for h in range(2):
                        act.wait_ge(sem(f"x_done{h}"), 1 + i * QP + q + 1)
                        act.activation((xr, xi)[h][:, q, :], pb[:, 4 + h, 0:N], ACT.Copy).then_inc(sem(f"x_out{h}"), 1)
                for t in range(2):
                    act.wait_ge(sem(f"block_done{t}"), g_fill[t] + i + 1)
                    act.activation(sg[:, bass.ds(i * 4 + 2 * t, 2), :], pb[:, 2 * t:2 * t + 2, 0:N], ACT.Sigmoid)\
                        .then_inc(sem("g_out"), 1)
                    if t == 0:
                        act.wait_ge(sem("c_done"), 1 + i)
                        act.activation(at(CCUR, 256), at(ALLW, KC, 512)[:, bass.ds(i, 1), 256:512], ACT.Copy)\
                            .then_inc(sem("ccur_ready"), 1)
            high_half(w_high, GLU_PLAN[0], glu_fill[0], 0, 2 * GLU_AT)
            act.wait_ge(sem("ys_done"), 1 + KC)
            act.wait_ge(sem("rot_done"), 1 + KC)
            for half in range(2):
                part = slice(half * 4 * N, (half + 1) * 4 * N)
                act.activation(u_full[:, part], at(UT, KC * N)[:, part], ACT.Gelu_apprx_tanh).then_inc(sem("gelu_done"), 1)
                act.wait_ge(sem("gelu_done"), half + 1)
                act.activation(u_high[:, part], u_full[:, part], ACT.Copy).then_inc(sem("u_high"), 1)
            high_half(w_high, GLU_PLAN[0], glu_fill[0], 1, 2 * GLU_AT + 1)
            act.wait_ge(sem("fin_t"), 1)
            act.activation(at(FO, 512, rows=PAIRS), pb[0:PAIRS, 5, :], ACT.Copy).then_inc(sem("fin_out"), 1)
            act.wait_ge(sem("fin_out"), 1)
            for n, name in enumerate(("re_p", "im_p", "re_s", "im_s")):
                act.dma_start(o_[name][0, 0].rearrange("(r g) p -> r (g p)", g=2), at(FO + n * P, P, rows=PAIRS))\
                    .then_inc(sem("fin_dma"), 16)

            def glu_gates(q):
                act.wait_ge(sem("block_done2"), glu_fill[0] + q + 1)
                act.wait_ge(sem("glu_m"), 1 + q)
                act.activation(at(SBT2, 4, N), pb[:, 4:8, 0:N], ACT.Sigmoid).then_inc(sem("glub_out"), 1)

            high(w_high, 0, glu_fill[1], GLU_AT + 1)
            glu_gates(0)
            high(w_high, 2, glu_fill[0] + 1, GLU_AT + 2)
            act.wait_ge(sem("xc_done"), 1)
            act.activation(at(SQ, KC, CW), vp[:, :, 0:CW], ACT.Square).then_inc(sem("sq_ln"), 1)
            high(w_high, 0, glu_fill[1] + 1, GLU_AT + 3)
            glu_gates(1)
            high(w_high, 2, glu_fill[0] + 2, GLU_AT + 4)
            act.wait_ge(sem("var_read"), 1)
            act.activation(at(MU + CW, CW), at(MU, CW), ACT.Sqrt).then_inc(sem("sd_ln"), 1)
            high(w_high, 0, glu_fill[1] + 2, GLU_AT + 5)
            glu_gates(2)
            high(w_high, 2, glu_fill[0] + 3, GLU_AT + 6)
            act.wait_ge(sem("z_done"), 1)
            act.activation(at(SQ, KC, CW), vp[:, :, 0:CW], ACT.Sigmoid).then_inc(sem("z_sig"), 1)
            high(w_high, 0, glu_fill[1] + 3, GLU_AT + 7)
            glu_gates(3)
            for first, turns, slots_, fills in ((CO_AT, 2, CO_PLAN, co_fill), (WO_AT, 4, WO_PLAN, wo_fill)):
                with act.Fori(0, turns) as i:
                    for t in range(2):
                        high(w_high, slots_[t], i + fills[t], i * 2 + (first + t))
            def ht_ready(g):
                act.wait_ge(sem("wo_out0"), 1 + g + 1)
                act.wait_ge(sem("wo_out1"), 1 + g + 1)

            squares(ht, at(SG, KD, N), ht_ready, sem("sq2"))
            for n in range(NT * 4):
                if n == 1:
                    act.wait_ge(sem("v2"), 1)
                    act.activation(at(RT + N, N), at(RT, N), ACT.Sqrt).then_inc(sem("sd2"), 1)
                j, g = divmod(n, 4)
                act.wait_ge(sem("hr_t"), n + 1)
                act.activation(at(HROWS, NT, D, rows=TOK)[:, j, g * 512:(g + 1) * 512], pb[0:TOK, n % 4, :],
                               ACT.Copy).then_inc(sem("hr_out"), 1)
            for j in range(NT):
                act.wait_ge(sem("hr_out"), 4 * (j + 1))
                act.dma_start(h_dram[j * TOK:(j + 1) * TOK, :], at(HROWS, NT, D, rows=TOK)[:, j, :]).then_inc(sem("h_out"), 16)
            act.wait_ge(sem("lgt"), 1)
            act.activation(at(LGT, N, rows=36), pb[0:36, 5, 0:N], ACT.Copy).then_inc(sem("lgt_out"), 1)
            for n in range(NT * 4):
                j, g = divmod(n, 4)
                act.wait_ge(sem("xnt_t"), n + 1)
                act.activation(at(XNT, NT, D, rows=TOK)[:, j, g * 512:(g + 1) * 512], pb[0:TOK, n % 4, :],
                               ACT.Copy).then_inc(sem("xnt_act"), 1)
            act.wait_ge(sem("rt_g"), 1)
            act.activation(at(RT + 120, 12, rows=TOK), at(RT + 108, 12, rows=TOK), ACT.Exp).then_inc(sem("rt_ge"), 1)
            act.wait_ge(sem("rt_d"), 1)
            act.activation(at(RT + 156, 3, rows=TOK), at(RT + 153, 3, rows=TOK), ACT.Exp).then_inc(sem("rt_de"), 1)
            xg = at(XG, KD, XW_COLS)
            act.wait_ge(sem("h_out"), 48)
            for k in range(KD):
                act.wait_ge(sem("xg_mm0"), k + 1)
                act.activation(xg[:, k, 0:N], pb[:, 4 + k % 2, 0:N], ACT.Copy).then_inc(sem("xg_act"), 1)
            act.wait_ge(sem("route_ints"), 1)
            y = at(Y, KD, XW_COLS)

            def expert(e):
                cnt = act.value_load(at(CNTI, EXPERTS, rows=1).bitcast(I32)[0:1, bass.ds(e, 1)], min_val=0, max_val=N)

                def narrow():
                    off = first_slot(act, e, False)
                    half1, g, s, half2 = (at(HID + 256 * n, FE, rows=NARROW) for n in range(4))
                    act.wait_ge(sem("block_done2"), exp_fill[0] + e + 1)
                    act.activation(half1, pb[NARROW:2 * NARROW, 4, 0:FE], ACT.Copy).then_inc(sem("gate_half"), 1)
                    act.wait_ge(sem("gate_sum"), e + 1)
                    act.activation(s, g, ACT.Sigmoid).then_inc(sem("sig_done"), 1)
                    act.wait_ge(sem("block_done0"), exp_fill[1] + e + 1)
                    act.activation(half2, pb[NARROW:2 * NARROW, 5, 0:FE], ACT.Copy).then_inc(sem("up_half"), 1)
                    act.wait_ge(sem("hid_t"), e + 1)
                    act.activation(at(HIDT, 2 * DOWN_N), pb[:, 6, 0:2 * DOWN_N], ACT.Copy).then_inc(sem("hid_copied"), 1)
                    act.wait_ge(sem("down_done"), 1 + e * KD + 8)
                    act.activation(y[:, 0:8, bass.ds(off, NARROW)].rearrange("p (b c) n -> p b c n", c=4),
                                   pb[:, 0:2, 0:4 * DOWN_N].rearrange("p b (c n) -> p b c n", n=DOWN_N)[:, :, :, 0:NARROW],
                                   ACT.Copy).then_inc(sem("down_act"), 8)

                def wide():
                    off = first_slot(act, e, True)
                    act.wait_ge(sem("block_done2"), exp_fill[0] + e + 1)
                    act.activation(at(HID, 2, WIDE), pb[:, 4:6, 0:WIDE], ACT.Sigmoid).then_inc(sem("sig_done"), 1)
                    act.sem_inc(sem("gate_half"), 1)
                    act.sem_inc(sem("up_half"), 1)
                    act.sem_inc(sem("hid_copied"), 1)
                    for c in range(8):
                        act.wait_ge(sem("down_done"), 1 + e * KD + c + 1)
                        act.activation(y[:, c, bass.ds(off, WIDE)], pb[:, c % 2, 0:WIDE], ACT.Copy)\
                            .then_inc(sem("down_act"), 1)

                with act.If(cnt < NARROW + 1):
                    narrow()
                with act.Else():
                    wide()

            with act.Fori(0, 1) as e:
                expert(e)
            act.wait_ge(sem("xg_mm1"), KD)
            gf = at(GF, D, rows=TOK)
            act.dma_start(gf, i_["norm_final_g"].unsqueeze(0).to_broadcast([TOK, D])).then_inc(sem("gf_in"), 16)
            with act.Fori(1, EXPERTS) as e:
                expert(e)

            for n in range(0, 4 * ST, 2):
                rows = min(P, SLOTS - n // 4 * P)
                act.wait_ge(sem("row_t"), n + 1)
                act.activation(at(n * 512, 512, rows=rows), pb[0:rows, n % 8, :], ACT.Copy).then_inc(sem("row_act"), 1)
            yg = at(YG, NT, 2, D, rows=TOK)
            act.wait_ge(sem("row_dve"), 2 * ST)
            for j in range(NT):
                act.wait_ge(sem("sum_done"), j + 1)
                act.activation(pb[0:TOK, 0:4, :], yg[:, j, 0, :].rearrange("p (a b) -> p a b", b=512), ACT.Square,
                               accum_out=at(RT + 4 * j, 1, rows=TOK)).then_inc(sem("ss_done"), 1)
                act.wait_ge(sem("vf"), j + 1)
                act.activation(at(RT + 4 * j + 1, 1, rows=TOK), at(RT + 4 * j, 1, rows=TOK), ACT.Sqrt).then_inc(sem("sdf"), 1)
                act.wait_ge(sem("scale_done"), j + 1)
                act.wait_ge(sem("gained"), j + 1)
                act.activation(yg[:, j, 0, :], yg[:, j, 1, :], ACT.Copy, scale=at(RT + 4 * j + 1, 1, rows=TOK))\
                    .then_inc(sem("y_done"), 1)
            act.wait_ge(sem("vout"), 32)
            act.wait_ge(sem("fin_dma"), 64)

        @block.vector
        def _(dve):
            for name in FIRST["dve"]:
                dve.sem_inc(sem(name), 1)
            v = nc.vector
            chain = Chain(dve, sem("dve_chain"))
            dve.wait_ge(sem("ld_in"), 16)
            v.tensor_copy(at(ROWS + P, 2, PS, rows=PAIRS), at(LD, 2, rows=PAIRS).unsqueeze(2).to_broadcast([PAIRS, 2, PS]))\
                .then_inc(sem("dt_rows"), 1)
            for m in range(1, KD // 2, 2):
                dve.wait_ge(sem("xt_t"), m + 1)
                v.tensor_copy(xt[:, 2 * m:2 * m + 2, :], pb[:, 2:4, 0:N]).then_inc(sem("xt_dve"), 1)

            def root(total, size, var, scale, v_sem, sd_sem, extra=None):
                vv, sd, tt = var
                chain(v.tensor_scalar(vv, total, scale, EPS, ALU.mult, ALU.add))
                v_sem_ins = v.tensor_copy(tt, vv)
                v_sem_ins.then_inc(v_sem, 1)
                dve.wait_ge(sd_sem[0], sd_sem[1])
                chain(v.reciprocal(sd, sd))
                chain(v.tensor_tensor(tt, sd, sd, ALU.mult))
                chain(v.tensor_tensor(tt, tt, vv, ALU.mult))
                chain(v.tensor_scalar(tt, tt, -0.5, 1.5, ALU.mult, ALU.add))
                chain(v.tensor_tensor(sd, sd, tt, ALU.mult))
                return sd

            dve.wait_ge(sem("ms1"), 1)
            r = root(pb[:, 5, 0:N], N, [at(SBT + n * N, N) for n in range(3)], 1.0 / D, sem("v1"), (sem("sd1"), 1))
            dve.wait_ge(sem("cv_out"), 1)
            for k in range(KD):
                v.scalar_tensor_tensor(xn[:, k, :], xt[:, k, :], cv[:, c_mix + k:c_mix + k + 1], r, ALU.mult, ALU.mult)\
                    .then_inc(sem("xn_ready"), 1)

            dt, lrdt, mag = at(SPA, 32), at(SPA + 32, 32), at(MAG, 32)
            th, kf, ang = at(SPA + 64, 8, 32), at(SPA + 1280, 256), at(SPA + 512, 256)
            sn, cs = at(SPA + 768, 8, 32), at(SPA + 1024, 8, 32)
            lr, li = cv[:, c_lr:c_lr + 32], cv[:, c_li:c_li + 32]
            dve.wait_ge(sem("dt_exp"), 1)
            v.tensor_tensor(lrdt, lr, dt, ALU.mult).then_inc(sem("lrdt"), 1)
            chain(v.tensor_tensor(th[:, 0, :], li, dt, ALU.mult))
            for k in range(1, 8):
                chain(v.tensor_scalar(th[:, k, :], th[:, 0, :], float(2 ** k), None, ALU.mult))
            thf = at(SPA + 64, 256)
            chain(v.tensor_scalar(kf, thf, 1 / (2 * math.pi), ROUND, ALU.mult, ALU.add))
            chain(v.tensor_scalar(kf, kf, ROUND, None, ALU.subtract))
            chain(v.scalar_tensor_tensor(ang, kf, -TWO_PI_1, thf, ALU.mult, ALU.add))
            chain(v.scalar_tensor_tensor(ang, kf, -TWO_PI_2, ang, ALU.mult, ALU.add))
            chain(v.scalar_tensor_tensor(ang, kf, -TWO_PI_3, ang, ALU.mult, ALU.add))
            v.tensor_scalar(ang, ang, 3.1415925, -3.1415925, ALU.min, ALU.max).then_inc(sem("angles"), 1)
            dve.wait_ge(sem("sines"), 2)
            csf = at(SPA + 1024, 256)
            chain(v.tensor_tensor(csf, csf, csf, ALU.mult))
            chain(v.tensor_scalar(csf, csf, -2.0, 1.0, ALU.mult, ALU.add))
            dve.wait_ge(sem("mag"), 1)
            w = [at(SPA + 1536 + 32 * n, 32) for n in range(12)]
            ar, ai, t1, t2, den, nr, cr, ci = w[:8]
            chain(v.tensor_tensor(ar, mag, cs[:, 0, :], ALU.mult))
            chain(v.tensor_tensor(ai, mag, sn[:, 0, :], ALU.mult))
            s_r, s_i = cv[:, c_sr:c_sr + 32], cv[:, c_si:c_si + 32]
            for out, p1, q1, p2, q2, op in ((at(INJ, 32), ar, s_r, ai, s_i, ALU.subtract),
                                            (at(INJ + 32, 32), ar, s_i, ai, s_r, ALU.add),
                                            (den, lr, lr, li, li, ALU.add)):
                chain(v.tensor_tensor(t1, p1, q1, ALU.mult))
                chain(v.tensor_tensor(t2, p2, q2, ALU.mult))
                chain(v.tensor_tensor(out, t1, t2, op))
            chain(v.tensor_scalar(nr, ar, 1.0, None, ALU.subtract))
            chain(v.reciprocal(den, den))
            for out, p1, q1, p2, q2, op in ((cr, nr, lr, ai, li, ALU.add), (ci, ai, lr, nr, li, ALU.subtract)):
                chain(v.tensor_tensor(t1, p1, q1, ALU.mult))
                chain(v.tensor_tensor(t2, p2, q2, ALU.mult))
                chain(v.tensor_tensor(t1, t1, t2, op))
                chain(v.tensor_tensor(out, t1, den, ALU.mult))
            br, bi = at(BR, PAIRS, HC), at(BR + 512, PAIRS, HC)
            crb, cib = (x.unsqueeze(2).to_broadcast([P, PAIRS, HC]) for x in (cr, ci))
            g1, g2 = at(SPA, PAIRS, HC), at(SPA + 1792, PAIRS, HC)
            par_i = at(PAR, 1).bitcast(I32)
            dve.wait_ge(sem("consts"), 5)
            dve.wait_ge(sem("bc_in"), 16 * 5)
            first = v.memset(at(EL, 2048), 0.0)
            chain(first)
            for base in (0, 1024):
                chain(v.memset(at(EL + base, PAIRS, 16)[:, :, 0:1], 1.0))
                tr, ti = at(EL + base, PAIRS, 16), at(EL + base + 512, PAIRS, 16)
                for lv in range(4):
                    n = 2 ** lv
                    k = lv + (4 if base else 0)
                    kr, ki = (x[:, k, :].unsqueeze(2).to_broadcast([P, PAIRS, n]) for x in (cs, sn))
                    m1, m2 = at(SPA + 1792, PAIRS, n), at(SPA + 2048, PAIRS, n)
                    for dst, p1, p2, op in ((tr, kr, ki, ALU.subtract), (ti, ki, kr, ALU.add)):
                        chain(v.tensor_tensor(m1, tr[:, :, 0:n], p1, ALU.mult))
                        chain(v.tensor_tensor(m2, ti[:, :, 0:n], p2, ALU.mult))
                        chain(v.tensor_tensor(dst[:, :, n:2 * n], m1, m2, op))
            chain(v.memset(at(BBP, 2048), 0.0))
            for h, (p1, q1, p2, q2, op) in enumerate(((crb, br, cib, bi, ALU.subtract), (crb, bi, cib, br, ALU.add))):
                chain(v.tensor_tensor(g1, q1, p1, ALU.mult))
                chain(v.tensor_tensor(g2, q2, p2, ALU.mult))
                bb = at(BBP + 1024 * h, PAIRS, 32)
                for half in range(2):
                    rows = slice(64 * half, 64 * half + 64)
                    chain(v.tensor_tensor(bb[rows, :, HC * half:HC * half + HC], g1[rows], g2[rows], op))
            chain(v.tensor_scalar(par_i, par_i, 4, 1, ALU.logical_shift_right, ALU.bitwise_and))
            odd, even = at(PAR + 1, 1), at(PAR + 2, 1)
            chain(v.tensor_copy(odd, par_i))
            chain(v.tensor_scalar(even, odd, -1.0, 1.0, ALU.mult, ALU.add))
            for h in range(2):
                src = at(CR + 512 * h, KC, PS)
                for half, mask in enumerate((even, odd)):
                    chain(v.tensor_scalar(at(CPAD + 1024 * h, KC, P)[:, :, PS * half:PS * half + PS], src, mask,
                                          -1.0 if h else 1.0, ALU.mult, ALU.mult))
            v.memset(at(FIN, 128), 0.0).then_inc(sem("bb_ready"), 1)

            dve.wait_ge(sem("cache_out"), 1)
            with dve.Fori(0, 4) as i:
                dve.wait_ge(sem("vb_out"), 1 + i + 1)
                dve.wait_ge(sem("block_done1"), v_fill[1] + i + 1)
                sb = at(SBT, 2, N)
                v.tensor_tensor(vp[:, bass.ds(i * 2, 2), PAD:PAD + TP], pb[:, 0:2, 0:TP], sb[:, :, 0:TP], ALU.mult)
                v.tensor_tensor(vp[:, bass.ds(i * 2, 2), 2 * PAD + TP:VW], pb[:, 0:2, TP:N], sb[:, :, TP:N], ALU.mult)\
                    .then_inc(sem("v_done"), 1)
            dve.wait_ge(sem("allw_out"), KC)
            v.memset(at(W, 1), 0.0).then_inc(sem("prep_done"), 1)
            dve.wait_ge(sem("vout_copied"), 2)
            dve.wait_ge(sem("v_done"), 1 + 4)
            dve.wait_ge(sem("vp_pad"), 1)
            v.memset(at(W + 1, 1), 0.0).then_inc(sem("w_free"), 1)

            xr, xi = at(XRI, QP, N), at(XRI + QP * N, QP, N)
            er, ei = at(E, QP, N), at(E + QP * N, QP, N)
            wr_, wi_ = at(W, QP, N), at(W + QP * N, QP, N)
            tt = at(T, QP, N)
            fin = at(FIN, 2, 2, PAIRS)
            acc = at(ACC, CW)
            flat = lambda off: at(off, QP * N)
            with dve.Fori(0, KC) as i:
                chain.enter(i, 48)

                def turn(dst, a1, b1, a2, b2, op):
                    v.tensor_tensor(dst, a1, b1, ALU.mult).then_inc(sem("dve_chain"), 1)
                    chain.n += 1
                    chain(v.tensor_tensor(tt, a2, b2, ALU.mult))
                    chain(v.tensor_tensor(dst, dst, tt, op))

                dve.wait_ge(sem("x_out0"), 1 + i * QP + QP)
                dve.wait_ge(sem("x_out1"), 1 + i * QP + QP)
                dve.wait_ge(sem("tab_ready"), i * 4 + 4)
                dve.wait_ge(sem("c_done"), 1 + i)
                turn(wr_, xr, er, xi, ei, ALU.add)
                turn(wi_, xi, er, xr, ei, ALU.subtract)
                for h, ww in enumerate((wr_, wi_)):
                    col = ww[:, :, TP:TP + 1]
                    chain(v.tensor_tensor(col, col, at(INJ + 32 * h, PAIRS)[:, bass.ds(i * QP, QP)].unsqueeze(2), ALU.add))
                for h in range(2):
                    v.tensor_tensor_scan(flat(XRI + h * QP * N), flat(DEC), flat(W + h * QP * N), 0.0, ALU.mult, ALU.add)\
                        .then_inc(sem("dve_chain"), 1)
                    chain.n += 1
                dve.wait_ge(sem("dve_chain"), chain.turn + chain.n)
                turn(wr_, xr, er, xi, ei, ALU.subtract)
                turn(wi_, xi, er, xr, ei, ALU.add)
                for h, ww in enumerate((wr_, wi_)):
                    ins = v.tensor_scalar(fin[:, :, h, bass.ds(i * QP, QP)], ww[:, :, TP - 1:N:TS].rearrange("p q t -> p t q"),
                                          1.0, None, ALU.mult)
                    ins.then_inc(sem("h_ready" if h else "dve_chain"), 1)
                chain.n += 1
                dve.wait_ge(sem("h_ready"), i + 1)
                src = vp[:, bass.ds(i, 1), :]
                a1 = acc.unsqueeze(1)

                def wk(k):
                    return cv[:, bass.ds(i + (c_cw + k * KC), 1)]

                v.memset(at(PAR + 3, 1), 0.0).then_inc(sem("rot_done"), 1)
                sums = (a1, at(ACC2, CW).unsqueeze(1))

                def step(ins):
                    ins.then_inc(sem("dve_chain"), 1)
                    chain.n += 1

                step(v.tensor_scalar(sums[0], src[:, :, 0:CW], wk(0), cv[:, bass.ds(i + c_cb, 1)], ALU.mult, ALU.add))
                step(v.tensor_scalar(sums[1], src[:, :, 1:1 + CW], wk(1), None, ALU.mult))
                for k in range(2, TAPS):
                    if k == 20:
                        dve.wait_ge(sem("c_done"), 1 + i + 1)
                        v.scalar_tensor_tensor(ut[:, bass.ds(i, 1), :], ut[:, bass.ds(i, 1), :],
                                               cv[:, bass.ds(i + c_ds, 1)], pb[:, 6:7, 0:N], ALU.mult, ALU.add)\
                            .then_inc(sem("ys_done"), 1)
                    dve.wait_ge(sem("dve_chain"), chain.turn + (chain.n - 1))
                    s_ = sums[k % 2]
                    step(v.scalar_tensor_tensor(s_, src[:, :, k:k + CW], wk(k), s_, ALU.mult, ALU.add))
                dve.wait_ge(sem("dve_chain"), chain.turn + chain.n)
                v.tensor_tensor(vp[:, bass.ds(i, 1), 0:CW], sums[0], sums[1], ALU.add).then_inc(sem("conv_done"), 1)
            chain.leave(KC)

            sb = at(SBT2, 4, N)
            dve.wait_ge(sem("g_out"), 1 + 16)

            m_all = m_full[:, :].rearrange("p (k n) -> p k n", n=N)

            def glu_products(q):
                dve.wait_ge(sem("block_done0"), glu_fill[1] + q + 1)
                dve.wait_ge(sem("glub_out"), 1 + q + 1)
                v.tensor_tensor(sb, pb[:, 0:4, 0:N], sb, ALU.mult).then_inc(sem("glua_out"), 1)
                dve.wait_ge(sem("glua_out"), 1 + q + 1)
                quad = bass.ds(q * 4, 4)
                v.tensor_tensor(m_all[:, quad, :], sb, sg[:, quad, :], ALU.mult).then_inc(sem("glu_m"), 1)

            glu_products(0)
            mu, sd, t3, t4 = (at(MU + n * CW, CW) for n in range(4))
            dve.wait_ge(sem("mean_done"), 1)
            v.tensor_scalar(mu, pb[:, 7, 0:CW], 1.0 / DC, None, ALU.mult).then_inc(sem("mu_done"), 1)
            dve.wait_ge(sem("mu_done"), 1)
            dve.wait_ge(sem("conv_done"), KC)
            v.tensor_tensor(vp[:, :, 0:CW], vp[:, :, 0:CW], mu.unsqueeze(1).to_broadcast([P, KC, CW]), ALU.subtract)\
                .then_inc(sem("xc_done"), 1)
            glu_products(1)
            dve.wait_ge(sem("var_done"), 1)
            v.tensor_scalar(mu, pb[:, 4, 0:CW], 1.0 / DC, EPS, ALU.mult, ALU.add).then_inc(sem("var_read"), 1)
            dve.wait_ge(sem("sd_ln"), 1)
            chain(v.reciprocal(sd, sd))
            chain(v.tensor_tensor(t3, sd, sd, ALU.mult))
            chain(v.tensor_tensor(t3, t3, mu, ALU.mult))
            chain(v.tensor_scalar(t3, t3, -0.5, 1.5, ALU.mult, ALU.add))
            chain(v.tensor_tensor(sd, sd, t3, ALU.mult))
            dve.wait_ge(sem("sq_ln"), 1)
            chain(v.tensor_tensor(vp[:, :, 0:CW], vp[:, :, 0:CW], sd.unsqueeze(1).to_broadcast([P, KC, CW]), ALU.mult))
            for c in range(KC):
                chain(v.tensor_scalar(vp[:, c, 0:CW], vp[:, c, 0:CW], cv[:, c_lg + c:c_lg + c + 1],
                                      cv[:, c_lb + c:c_lb + c + 1], ALU.mult, ALU.add))
            v.memset(at(PAR + 4, 1), 0.0).then_inc(sem("z_done"), 1)
            dve.wait_ge(sem("z_sig"), 1)
            sq = at(SQ, KC, CW)
            yb = y_full[:, :].rearrange("p (k n) -> p k n", n=N)
            chain(v.tensor_tensor(yb[:, :, 0:TP], vp[:, :, 0:TP], sq[:, :, 0:TP], ALU.mult))
            chain(v.tensor_tensor(yb[:, :, TP:N], vp[:, :, SMP:CW], sq[:, :, SMP:CW], ALU.mult))
            chain(v.tensor_scalar(y_high[:, :], y_full[:, :], 1.0, None, ALU.mult))
            v.tensor_tensor(y_low[:, :], y_full[:, :], y_high[:, :], ALU.subtract).then_inc(sem("yb_done"), 1)
            with dve.Fori(2, 4) as i:
                glu_products(i)
            dve.wait_ge(sem("glu_m"), 1 + 4)
            with dve.Fori(0, 2) as i:
                chain.enter(i, 4)
                for t in range(2):
                    q = bass.ds(i * 8 + 4 * t, 4)
                    mh, ml, mf = (x[:, :].rearrange("p (k n) -> p k n", n=N)[:, q, :] for x in (m_high, m_low, m_full))
                    qb = bass.ds(i * 8 + 4 * t + KD, 4)
                    dve.wait_ge(sem(f"block_done{1 + t}"), co_fill[t] + i + 1)
                    v.tensor_tensor(sb, pb[:, 4 * t:4 * t + 4, 0:N], sg[:, qb, :], ALU.mult).then_inc(sem(f"co_out{t}"), 1)
                    dve.wait_ge(sem(f"co_out{t}"), 1 + i + 1)
                    chain(v.tensor_tensor(mf, mf, sb, ALU.add))
                    ins = v.tensor_scalar(mh, mf, 1.0, None, ALU.mult)
                    if t == 0:
                        chain(ins)
                        chain(v.tensor_tensor(ml, mf, mh, ALU.subtract))
                    else:
                        ins.then_inc(sem("m_high"), 1)
                        dve.wait_ge(sem("m_high"), i + 1)
                        v.tensor_tensor(ml, mf, mh, ALU.subtract).then_inc(sem("m_low"), 1)
            chain.leave(2)
            dve.wait_ge(sem("ht_in"), 16)
            with dve.Fori(0, 4) as i:
                for t in range(2):
                    q = bass.ds(i * 4 + 2 * t, 2)
                    dve.wait_ge(sem(f"block_done{t}"), wo_fill[t] + i + 1)
                    v.tensor_tensor(ht[:, q, :], pb[:, 2 * t:2 * t + 2, 0:N], ht[:, q, :], ALU.add)\
                        .then_inc(sem(f"wo_out{t}"), 1)
            dve.wait_ge(sem("ms2"), 1)
            r = root(pb[:, 4, 0:N], N, [at(RT + n * N, N) for n in range(3)], 1.0 / D, sem("v2"), (sem("sd2"), 1))
            for k in range(KD):
                v.scalar_tensor_tensor(xn[:, k, :], ht[:, k, :], cv[:, c_ffn + k:c_ffn + k + 1], r, ALU.mult, ALU.mult)\
                    .then_inc(sem("xn2_ready"), 1)

            def rt(off, *shape):
                return at(RT + off, *shape, rows=TOK)

            def bc(x, n):
                return x.unsqueeze(2).to_broadcast([TOK, NT, n])

            dve.wait_ge(sem("xn2_ready"), KD)
            rev, iot = at(REV, EXPERTS, rows=TOK), at(IOT, SLOTS, rows=TOK)
            chain(v.tensor_copy(rev, rev.bitcast(I32)))
            dve.wait_ge(sem("iota_done"), 1)
            chain(v.tensor_copy(iot, iot.bitcast(I32)))
            lg, gl = rt(0, NT, 36), rt(108, NT, EG)
            ex, gm, eq4, wm = rt(120, NT, EG), rt(132, NT), rt(136, NT, EG), rt(148, NT)
            dif, ed, pg, v1, v2 = (rt(o, NT) for o in (153, 156, 160, 172, 176))
            w1, w2 = (at(GW_T + o, NT, rows=TOK) for o in (0, NT))
            lm, o1, o2, eq, a = (rt(180 + 0, NT, 32), rt(276, NT, 32), rt(372, NT, 32), rt(468, NT, 32), rt(600, NT, 32))
            msk, sl, off, incl, one32 = rt(700, NT, 32), rt(800, NT, 32), at(RT + 900, 32), at(RT + 932, 32), at(RT + 964, 32)

            def best(x, n, m, e, onehot):
                chain(v.tensor_reduce(m, x, AX, ALU.max))
                chain(v.tensor_tensor(e, x, bc(m, n), ALU.is_equal))
                chain(v.tensor_tensor(e, e, rev[:, 0:n].unsqueeze(1).to_broadcast([TOK, NT, n]), ALU.mult))
                chain(v.tensor_reduce(wm, e, AX, ALU.max))
                chain(v.tensor_tensor(onehot, e, bc(wm, n), ALU.is_equal))

            dve.wait_ge(sem("logits"), 1)
            dve.wait_ge(sem("wr_in"), 64)
            chain(v.tensor_tensor(lg, pb[0:TOK, 6, 0:108].rearrange("p (j c) -> p j c", c=36),
                                  at(RB, 36, rows=TOK).unsqueeze(1).to_broadcast([TOK, NT, 36]), ALU.add))
            best(lg[:, :, 0:EG], EG, gm, eq4, eq4)
            v.tensor_tensor(gl, lg[:, :, 0:EG], bc(gm, EG), ALU.subtract).then_inc(sem("rt_g"), 1)
            chain(v.tensor_copy(msk.rearrange("p j (g e) -> p j g e", e=EPG), eq4.unsqueeze(3).to_broadcast([TOK, NT, EG, EPG])))
            chain(v.tensor_tensor(lm, lg[:, :, EG:36], msk, ALU.mult))
            chain(v.tensor_scalar(msk, msk, 1e30, 1e30, ALU.mult, ALU.subtract))
            chain(v.tensor_tensor(lm, lm, msk, ALU.add))
            best(lm, 32, v1, eq, o1)
            chain(v.scalar_tensor_tensor(lm, o1, -3e38, lm, ALU.mult, ALU.add))
            best(lm, 32, v2, eq, o2)
            v.tensor_tensor(dif, v2, v1, ALU.subtract).then_inc(sem("rt_d"), 1)
            v.tensor_tensor(a, o1, o2, ALU.add).then_inc(sem("assigned"), 1)
            dve.wait_ge(sem("rt_ge"), 1)
            chain(v.tensor_reduce(pg, ex, AX, ALU.add))
            dve.wait_ge(sem("rt_de"), 1)
            chain(v.tensor_scalar(w1, ed, 1.0, None, ALU.add))
            chain(v.tensor_tensor(w1, w1, pg, ALU.mult))
            chain(v.reciprocal(w1, w1))
            chain(v.tensor_tensor(w2, w1, ed, ALU.mult))
            chain(v.memset(one32, 1.0))
            dve.wait_ge(sem("ranks"), 1)
            chain(v.tensor_tensor_scan(incl, one32, pb[:, 7, 128:160], 0.0, ALU.mult, ALU.add))
            chain(v.tensor_tensor(off, incl, pb[:, 7, 128:160], ALU.subtract))
            v.tensor_copy(at(CNTI, 32, rows=1).bitcast(I32), pb[0:1, 7, 128:160])
            chain(v.tensor_copy(at(OFFI, 32, rows=1).bitcast(I32), at(RT + 900, 32, rows=1)))
            v.memset(at(PAR + 4, 1), 0.0).then_inc(sem("route_ints"), 1)
            chain(v.tensor_tensor(sl, pb[0:TOK, 7, 0:96].rearrange("p (j c) -> p j c", c=32),
                                  at(RT + 900, 32, rows=TOK).unsqueeze(1).to_broadcast([TOK, NT, 32]), ALU.add))
            sf = at(S1F, 2, NT, rows=TOK)
            for n, o in enumerate((o1, o2)):
                chain(v.tensor_tensor(eq, o, sl, ALU.mult))
                chain(v.tensor_reduce(sf[:, n, :], eq, AX, ALU.add))
            chain(v.tensor_copy(at(IDX, 2, NT, rows=TOK).bitcast(I32), sf))
            oh, tmp = at(OH, NT, SLOTS, rows=TOK), at(TMP, SLOTS, rows=TOK)
            for j in range(NT):
                chain(v.tensor_scalar(tmp, iot, sf[:, 0, j:j + 1], None, ALU.is_equal))
                chain(v.scalar_tensor_tensor(oh[:, j, :], iot, sf[:, 1, j:j + 1], tmp, ALU.is_equal, ALU.add))
            v.memset(at(PAR + 4, 1), 0.0).then_inc(sem("onehot"), 1)
            y = at(Y, KD, XW_COLS)
            n0 = chain.n

            def expert(e):
                chain.n = n0
                chain.enter(e, 2)
                cnt = dve.value_load(at(CNTI, EXPERTS, rows=1).bitcast(I32)[0:1, bass.ds(e, 1)], min_val=0, max_val=N)

                def narrow():
                    off = first_slot(dve, e, False)
                    half1, g, s, half2, h = (at(HID + 256 * n, FE, rows=NARROW) for n in range(5))
                    dve.wait_ge(sem("gate_half"), e + 1)
                    v.tensor_tensor(g, pb[0:NARROW, 4, 0:FE], half1, ALU.add).then_inc(sem("gate_sum"), 1)
                    dve.wait_ge(sem("sig_done"), e + 1)
                    chain(v.tensor_tensor(g, g, s, ALU.mult))
                    dve.wait_ge(sem("up_half"), e + 1)
                    chain(v.tensor_tensor(h, pb[0:NARROW, 5, 0:FE], half2, ALU.add))
                    v.tensor_tensor(h, h, g, ALU.mult).then_inc(sem("hid_done"), 1)
                    dve.wait_ge(sem("down_done"), 1 + e * KD + KD)
                    v.tensor_scalar(y[:, 8:KD, bass.ds(off, NARROW)].rearrange("p (b c) n -> p b c n", c=4),
                                    pb[:, 2:4, 0:4 * DOWN_N].rearrange("p b (c n) -> p b c n", n=DOWN_N)[:, :, :, 0:NARROW],
                                    1.0, None, ALU.mult).then_inc(sem("down_dve"), 8)

                def wide():
                    off = first_slot(dve, e, True)
                    s, t, h = (at(HID + 576 * n, 2, WIDE) for n in range(3))
                    dve.sem_inc(sem("gate_sum"), 1)
                    dve.wait_ge(sem("sig_done"), e + 1)
                    chain(v.tensor_tensor(t, pb[:, 4:6, 0:WIDE], s, ALU.mult))
                    dve.wait_ge(sem("block_done0"), exp_fill[1] + e + 1)
                    chain(v.tensor_tensor(t, t, pb[:, 6:8, 0:WIDE], ALU.mult))
                    v.tensor_copy(h, t).then_inc(sem("hid_done"), 1)
                    for c in range(8, KD):
                        dve.wait_ge(sem("down_done"), 1 + e * KD + c + 1)
                        v.tensor_scalar(y[:, c, bass.ds(off, WIDE)], pb[:, 2 + c % 2, 0:WIDE], 1.0, None, ALU.mult)\
                            .then_inc(sem("down_dve"), 1)

                with dve.If(cnt < NARROW + 1):
                    narrow()
                chain.n = n0
                with dve.Else():
                    wide()

            with dve.Fori(0, 1) as e:
                expert(e)
            xg = at(XG, KD, XW_COLS)
            dve.wait_ge(sem("h_out"), 48)
            for k in range(KD):
                dve.wait_ge(sem("xg_mm1"), k + 1)
                v.tensor_copy(xg[:, k, N:2 * N], pb[:, 6 + k % 2, 0:N]).then_inc(sem("xg_dve"), 1)
            with dve.Fori(1, EXPERTS) as e:
                expert(e)
            chain.leave(EXPERTS)

            for n in range(1, 4 * ST, 2):
                rows = min(P, SLOTS - n // 4 * P)
                dve.wait_ge(sem("row_t"), n + 1)
                v.tensor_copy(at(n * 512, 512, rows=rows), pb[0:rows, n % 8, :]).then_inc(sem("row_dve"), 1)
            yg = at(YG, NT, 2, D, rows=TOK)
            dve.wait_ge(sem("h_back"), 16)
            def scale(j):
                ss, sd_, t_ = (at(RT + 4 * j + n, 1, rows=TOK) for n in (0, 1, 3))
                dve.wait_ge(sem("ss_done"), j + 1)
                v.tensor_scalar(ss, ss, 1.0 / D, EPS, ALU.mult, ALU.add).then_inc(sem("vf"), 1)
                dve.wait_ge(sem("sdf"), j + 1)
                chain(v.reciprocal(sd_, sd_))
                chain(v.tensor_tensor(t_, sd_, sd_, ALU.mult))
                chain(v.tensor_tensor(t_, t_, ss, ALU.mult))
                chain(v.tensor_scalar(t_, t_, -0.5, 1.5, ALU.mult, ALU.add))
                v.tensor_tensor(sd_, sd_, t_, ALU.mult).then_inc(sem("scale_done"), 1)

            for j in range(NT):
                dve.wait_ge(sem(f"rows_in{j}"), 32)
                w1, w2 = (at(GW_T + NT * n + j, 1, rows=TOK) for n in range(2))
                chain(v.scalar_tensor_tensor(yg[:, j, 0, :], yg[:, j, 0, :], w1, at(HN, NT, D, rows=TOK)[:, j, :],
                                             ALU.mult, ALU.add))
                v.scalar_tensor_tensor(yg[:, j, 0, :], yg[:, j, 1, :], w2, yg[:, j, 0, :], ALU.mult, ALU.add)\
                    .then_inc(sem("sum_done"), 1)
                if j > 0:
                    scale(j - 1)
            scale(NT - 1)


_OUTS = {
    "y_prompt": (1, TP, D), "y_sample": (1, TS, D),
    "re_p": (1, 1, G, PS), "im_p": (1, 1, G, PS), "conv_p": (1, 1, PAD, DC),
    "re_s": (1, 1, G, PS), "im_s": (1, 1, G, PS), "conv_s": (1, 1, PAD, DC),
}


def kernel(**inputs):
    import numpy as np
    import concourse.bacc as bacc
    from concourse.bass_utils import run_bass_kernel_spmd as run

    nc = bacc.Bacc("TRN2", target_bir_lowering=False, num_devices=1)
    arrays, ins, outs = {}, {}, {}
    for name, a in inputs.items():
        a = np.ascontiguousarray(a)
        arrays["in_" + name] = a
        ins[name] = nc.dram_tensor("in_" + name, a.shape, mybir.dt.from_np(a.dtype), kind="ExternalInput").ap()
    for name, shape in _OUTS.items():
        outs[name] = nc.dram_tensor("out_" + name, shape, F32, kind="ExternalOutput").ap()
    xt_dram = nc.dram_tensor("xt_keep", (P, KD * N), F32, kind="Internal").ap()
    slots_dram = nc.dram_tensor("slot_rows", (SLOTS, D), F32, kind="Internal").ap()
    h_dram = nc.dram_tensor("h_keep", (N, D), F32, kind="Internal").ap()
    build(nc, ins, outs, xt_dram, h_dram, slots_dram)
    r = run(nc, [arrays], core_ids=[0])
    return tuple(r.results[0]["out_" + name] for name in _OUTS)
```
